# Optimizing a Trainium2 kernel written in Bass

```python
import math
import jax, jax.numpy as jnp
from jax import lax
import numpy as np

D_MODEL = 1024
BATCH = 1
SEQ = 256
DEPTH = 1
DEC_BATCH = 1
DEC_SEQ = 1024
PAST_LEN = 128

HEAD_DIM = 64
MIX_WIDTH = D_MODEL
ATTN_WIDTH = MIX_WIDTH // 2
GMLP_WIDTH = MIX_WIDTH - ATTN_WIDTH
N_ATTN_HEADS = ATTN_WIDTH // HEAD_DIM
N_GMLP_GROUPS = GMLP_WIDTH // HEAD_DIM
IN_PROJ_WIDTH = 3 * ATTN_WIDTH + 2 * GMLP_WIDTH
GMLP_CHUNK = 128
DILATED_BRANCHES = ((128, 1), (512, 4), (2048, 16))
ATTN_BLOCK = 64
N_REL_BUCKETS = 32
REL_MAX_DISTANCE = 1024
N_EXPERTS = 16
EC_CAPACITY_FACTOR = 2
D_FF_EXPERT = 2816
DEEPNORM_ALPHA = (2 * DEPTH) ** 0.25
DEEPNORM_BETA = (8 * DEPTH) ** -0.25
LN_EPS = 1e-5

kernel_name = 'hybrid_dilated_attn_gmlp_ec_moe_encoder'

def layer_norm(x, g, b):
    xf = x.astype(jnp.float32)
    mu = jnp.mean(xf, -1, keepdims=True)
    var = jnp.mean(jnp.square(xf - mu), -1, keepdims=True)
    y = (xf - mu) * lax.rsqrt(var + LN_EPS)
    return (y * g.astype(jnp.float32) + b.astype(jnp.float32)).astype(x.dtype)

def t5_bucket(rel):
    half = N_REL_BUCKETS // 2
    ret = np.where(rel > 0, half, 0)
    n = np.abs(rel)
    max_exact = half // 2
    large = max_exact + (np.log(np.maximum(n, 1) / max_exact) / np.log(REL_MAX_DISTANCE / max_exact) * (half - max_exact)).astype(np.int32)
    large = np.minimum(large, half - 1)
    return (ret + np.where(n < max_exact, n, large)).astype(np.int32)

def dilated_window_branch(q, k, v, rel_table, window, dilation):
    B, L, H, Dh = q.shape
    d = dilation
    W = window // 2 // d
    Lr = L // d
    blk = math.gcd(ATTN_BLOCK, Lr)
    nb = Lr // blk
    win = blk + 2 * W

    def to_residue(t):
        return t.reshape(B, Lr, d, H, Dh).transpose(0, 2, 3, 1, 4)

    qb = to_residue(q).reshape(B, d, H, nb, blk, Dh)
    pad = ((0, 0), (0, 0), (0, 0), (W, W), (0, 0))
    kp = jnp.pad(to_residue(k), pad)
    vp = jnp.pad(to_residue(v), pad)
    idx = np.arange(nb)[:, None] * blk + np.arange(win)[None, :]
    kw = kp[:, :, :, idx]
    vw = vp[:, :, :, idx]
    off = np.arange(win)[None, :] - W - np.arange(blk)[:, None]
    key_pos = idx - W
    valid = (np.abs(off) <= W)[None] & ((key_pos >= 0) & (key_pos < Lr))[:, None, :]
    bias = rel_table[t5_bucket(np.clip(off, -W, W) * d)]
    s = jnp.einsum('bdhnqc,bdhnkc->bdhnqk', qb, kw).astype(jnp.float32) * (HEAD_DIM ** -0.5)
    s = s + jnp.transpose(bias, (2, 0, 1)).astype(jnp.float32)[None, None, :, None]
    s = jnp.where(valid[None, None, None], s, -jnp.inf)
    m = jnp.max(s, -1, keepdims=True)
    p = jnp.exp(s - m)
    den = jnp.sum(p, -1, keepdims=True)
    o = jnp.einsum('bdhnqk,bdhnkc->bdhnqc', (p / den).astype(v.dtype), vw)
    lse = (m + jnp.log(den))[..., 0]
    o = o.reshape(B, d, H, Lr, Dh).transpose(0, 3, 1, 2, 4).reshape(B, L, H, Dh)
    lse = lse.reshape(B, d, H, Lr).transpose(0, 3, 1, 2).reshape(B, L, H)
    return o, lse

def dilated_attention(q, k, v, rel_table):
    outs, lses = [], []
    for window, dilation in DILATED_BRANCHES:
        o, lse = dilated_window_branch(q, k, v, rel_table, window, dilation)
        outs.append(o)
        lses.append(lse)
    w = jax.nn.softmax(jnp.stack(lses, 0), axis=0)
    return jnp.einsum('nblh,nblhc->blhc', w.astype(q.dtype), jnp.stack(outs, 0))

def gmlp_spatial_gating(u, vg, ln_g, ln_b, w_s, b_s):
    B, L, _ = u.shape
    vn = layer_norm(vg, ln_g, ln_b)
    vc = vn.reshape(B, L // GMLP_CHUNK, GMLP_CHUNK, N_GMLP_GROUPS, HEAD_DIM)
    vm = jnp.einsum('gpq,bnqgc->bnpgc', w_s, vc) + b_s.T[None, None, :, :, None]
    return u * vm.reshape(B, L, GMLP_WIDTH)

def hybrid_mixer(x, rel_table, w_in, b_in, gmlp_ln_g, gmlp_ln_b, gmlp_w_s, gmlp_b_s, w_out):
    B, L, _ = x.shape
    h = jnp.einsum('bld,de->ble', x, w_in) + b_in
    q, k, v, gu, gv = jnp.split(h, [ATTN_WIDTH, 2 * ATTN_WIDTH, 3 * ATTN_WIDTH, 3 * ATTN_WIDTH + GMLP_WIDTH], axis=-1)
    shp = (B, L, N_ATTN_HEADS, HEAD_DIM)
    attn = dilated_attention(q.reshape(shp), k.reshape(shp), v.reshape(shp), rel_table).reshape(B, L, ATTN_WIDTH)
    gm = gmlp_spatial_gating(jax.nn.gelu(gu), jax.nn.gelu(gv), gmlp_ln_g, gmlp_ln_b, gmlp_w_s, gmlp_b_s)
    return jnp.einsum('ble,ed->bld', jnp.concatenate([attn, gm], axis=-1), w_out)

def expert_choice_moe(x, w_router, w_gate, w_up, w_down):
    B, L, D = x.shape
    n = B * L
    xt = x.reshape(n, D)
    cap = EC_CAPACITY_FACTOR * n // N_EXPERTS
    aff = jax.nn.softmax((xt @ w_router).astype(jnp.float32), axis=-1)
    gates, idx = lax.top_k(aff.T, cap)
    xs = xt[idx]

    def expert(args):
        xe, wg, wu, wd = args
        return (jax.nn.silu(xe @ wg) * (xe @ wu)) @ wd

    ys = lax.map(expert, (xs, w_gate, w_up, w_down))
    ys = ys * gates[..., None].astype(ys.dtype)
    out = jnp.zeros_like(xt).at[idx.reshape(-1)].add(ys.reshape(-1, D))
    return out.reshape(B, L, D)

def encoder_trunk(x, rel_bias_table, w_in, b_in, gmlp_ln_g, gmlp_ln_b, gmlp_w_s, gmlp_b_s, w_out,
                  ln1_g, ln1_b, w_router, w_gate, w_up, w_down, ln2_g, ln2_b):
    for l in range(DEPTH):
        mix = hybrid_mixer(x, rel_bias_table, w_in[l], b_in[l], gmlp_ln_g[l], gmlp_ln_b[l],
                           gmlp_w_s[l], gmlp_b_s[l], w_out[l])
        x = layer_norm(DEEPNORM_ALPHA * x + mix, ln1_g[l], ln1_b[l])
        ffn = expert_choice_moe(x, w_router[l], w_gate[l], w_up[l], w_down[l])
        x = layer_norm(DEEPNORM_ALPHA * x + ffn, ln2_g[l], ln2_b[l])
    return x

def setup_inputs(seed: int = 0) -> dict:
    key = jax.random.key(seed)
    ks = jax.random.split(key, 20)
    f32 = jnp.float32
    nrm = lambda k, shape, s: jax.random.normal(k, shape, f32) * s
    return {
        'x_prompt': nrm(ks[0], (BATCH, SEQ, D_MODEL), 1.0),
        'x_sample': nrm(ks[1], (DEC_BATCH, DEC_SEQ, D_MODEL), 1.0),
        'rel_bias_table': nrm(ks[2], (N_REL_BUCKETS, N_ATTN_HEADS), 0.5),
        'w_in': nrm(ks[3], (DEPTH, D_MODEL, IN_PROJ_WIDTH), D_MODEL ** -0.5),
        'b_in': nrm(ks[4], (DEPTH, IN_PROJ_WIDTH), 0.02),
        'gmlp_ln_g': 1.0 + nrm(ks[5], (DEPTH, GMLP_WIDTH), 0.02),
        'gmlp_ln_b': nrm(ks[6], (DEPTH, GMLP_WIDTH), 0.02),
        'gmlp_w_s': nrm(ks[7], (DEPTH, N_GMLP_GROUPS, GMLP_CHUNK, GMLP_CHUNK), GMLP_CHUNK ** -0.5),
        'gmlp_b_s': 1.0 + nrm(ks[8], (DEPTH, N_GMLP_GROUPS, GMLP_CHUNK), 0.02),
        'w_out': nrm(ks[9], (DEPTH, MIX_WIDTH, D_MODEL), MIX_WIDTH ** -0.5 * DEEPNORM_BETA),
        'ln1_g': 1.0 + nrm(ks[10], (DEPTH, D_MODEL), 0.02),
        'ln1_b': nrm(ks[11], (DEPTH, D_MODEL), 0.02),
        'w_router': nrm(ks[12], (DEPTH, D_MODEL, N_EXPERTS), D_MODEL ** -0.5),
        'w_gate': nrm(ks[13], (DEPTH, N_EXPERTS, D_MODEL, D_FF_EXPERT), D_MODEL ** -0.5),
        'w_up': nrm(ks[14], (DEPTH, N_EXPERTS, D_MODEL, D_FF_EXPERT), D_MODEL ** -0.5),
        'w_down': nrm(ks[15], (DEPTH, N_EXPERTS, D_FF_EXPERT, D_MODEL), D_FF_EXPERT ** -0.5 * DEEPNORM_BETA),
        'ln2_g': 1.0 + nrm(ks[16], (DEPTH, D_MODEL), 0.02),
        'ln2_b': nrm(ks[17], (DEPTH, D_MODEL), 0.02),
    }

def reference(x_prompt, x_sample, rel_bias_table, w_in, b_in, gmlp_ln_g, gmlp_ln_b, gmlp_w_s, gmlp_b_s,
              w_out, ln1_g, ln1_b, w_router, w_gate, w_up, w_down, ln2_g, ln2_b):
    y_prompt = encoder_trunk(x_prompt, rel_bias_table, w_in, b_in, gmlp_ln_g, gmlp_ln_b, gmlp_w_s, gmlp_b_s,
                             w_out, ln1_g, ln1_b, w_router, w_gate, w_up, w_down, ln2_g, ln2_b)
    y_sample = encoder_trunk(x_sample, rel_bias_table, w_in, b_in, gmlp_ln_g, gmlp_ln_b, gmlp_w_s, gmlp_b_s,
                             w_out, ln1_g, ln1_b, w_router, w_gate, w_up, w_down, ln2_g, ln2_b)
    return (y_prompt, y_sample)


_drawn_inputs = setup_inputs


def setup_inputs(seed=0):
    import zlib

    import numpy as np

    out = dict(_drawn_inputs(seed))
    spreads = {}
    factors = {'b_in': 4.726,
     'gmlp_ln_g': 28.297,
     'gmlp_ln_b': 29.089,
     'gmlp_b_s': 32.613,
     'ln1_b': 2.676,
     'ln2_g': 8.137,
     'ln2_b': 8.21,
     'rel_bias_table': 5.874,
     'ln1_g': 2.688}
    for name, (base, spread) in spreads.items():
        noise = np.random.default_rng([zlib.crc32(name.encode()), seed]).standard_normal(out[name].shape)
        drawn = base * np.exp(spread * noise) if base else spread * noise
        out[name] = __import__('jax').numpy.asarray(drawn.astype(out[name].dtype))
    for name, factor in factors.items():
        out[name] = (out[name] * factor).astype(out[name].dtype)
    return out
```

```python
import math
from contextlib import ExitStack

import numpy as np
import concourse.bass as bass
from concourse import mybir

F32 = mybir.dt.float32
F32R = mybir.dt.float32r
U32 = mybir.dt.uint32
ALU = mybir.AluOpType
ACT = mybir.ActivationFunctionType
AX_X = mybir.AxisListType.X

P = 128
D = 1024
KT = D // P
L_PROMPT, L_SAMPLE = 256, 1024
TOKENS = L_PROMPT + L_SAMPLE
TILES = TOKENS // P
PT = L_PROMPT // P
HEADS, HD = 8, 64
AW = HEADS * HD
E_IN = 5 * AW
EXPERTS, FF = 16, 2816
FT = FF // P
CAP_P, CAP_S = 2 * L_PROMPT // EXPERTS, 2 * L_SAMPLE // EXPERTS
SLOTS = CAP_S + CAP_P
ALPHA = 2.0 ** 0.25
EPS = 1e-5
N_BUCKETS, MAX_DIST = 32, 1024
REL = 2 * L_SAMPLE
BIAS_W = L_SAMPLE - P + L_SAMPLE
MASKED = -1e30

PAIRS = FT // 2
GU_UNITS = 4 * PAIRS
DN_UNITS = PAIRS
UNITS = GU_UNITS + 2 * DN_UNITS
RING = 11
SPLIT = 6
UW = 1024


def relative_rows():
    rel = (L_SAMPLE - 1) - np.arange(REL)
    half = N_BUCKETS // 2
    n = np.abs(rel)
    max_exact = half // 2
    large = max_exact + (np.log(np.maximum(n, 1) / max_exact) / np.log(MAX_DIST / max_exact)
                         * (half - max_exact)).astype(np.int32)
    bucket = np.where(rel > 0, half, 0) + np.where(n < max_exact, n, np.minimum(large, half - 1))
    count = sum(((n <= w // 2) & (n % d == 0)).astype(np.int64) for w, d in ((128, 1), (512, 4), (2048, 16)))
    rows = np.zeros((N_BUCKETS + 1, REL), np.float32)
    rows[bucket, np.arange(REL)] = 1.0
    rows[N_BUCKETS] = np.where(count > 0, np.log(np.maximum(count, 1)), MASKED)
    return rows


def build(nc, a, outs):
    out_prompt, out_sample = outs
    w_in, w_out = a["w_in"][0], a["w_out"][0]
    w_gate, w_up, w_down = a["w_gate"][0], a["w_up"][0], a["w_down"][0]
    x1_d = nc.dram_tensor("x1_rows", (TOKENS, D), F32, kind="Internal").ap()
    acc_d = nc.dram_tensor("acc_rows", (TOKENS, D), F32, kind="Internal").ap()
    rel_d = nc.dram_tensor("rel_bias", (HEADS, REL), F32, kind="Internal").ap()

    def token_rows(prompt, sample, t):
        return prompt[0, t * P:(t + 1) * P, :] if t < PT else sample[0, (t - PT) * P:(t - PT + 1) * P, :]

    with ExitStack() as ctx:
        def sem(name):
            return ctx.enter_context(nc.semaphore(name))

        with nc.sbuf_tensor("arena", [P, 50176 + 2800], F32) as arena:
            pass
        raw = ctx.enter_context(nc.sbuf_tensor("raw_units", [P, RING, UW], F32))
        w_parts = ctx.enter_context(nc.sbuf_tensor("w_parts", [P, 2, SPLIT, UW], F32R))
        between = ctx.enter_context(nc.sbuf_tensor("between_parts", [P, 34816 - 11264 - 2 * SPLIT * UW], F32))
        xs_parts = ctx.enter_context(nc.sbuf_tensor("xs_parts", [P, 2, KT, SLOTS], F32R))
        h_parts = ctx.enter_context(nc.sbuf_tensor("h_parts", [P, 2, FT, SLOTS], F32R))
        HI, LO = 0, 1
        psum = ctx.enter_context(nc.psum_tensor("banks", [P, 8, 512], F32))

        def at(start, *shape):
            n = math.prod(shape)
            v = arena[:, start:start + n]
            if len(shape) == 2:
                v = v.rearrange("p (a b) -> p a b", a=shape[0])
            elif len(shape) == 3:
                v = v.rearrange("p (a b c) -> p a b c", a=shape[0], b=shape[1])
            return v

        R_LOW, R_WOUT, R_QKV, R_CAT, R_VN, R_SMALL = 0, 11264, 19456, 34816, 45056, 50176
        xT = at(R_LOW, KT, TOKENS)
        win = at(10240, 2, KT, AW)
        qT = at(R_QKV, 4, TOKENS)
        kT = at(R_QKV + 5120, 4, TOKENS)
        x_rows = at(R_QKV, TILES, D)
        v_rows = at(R_QKV + 10240, TILES, AW)
        rel_rows = at(R_QKV + 10240, REL)
        rel_bias = at(R_QKV + 10240 + REL, REL)
        ws_rows = at(R_QKV + 10240 + 2 * REL, 8, P)
        cat = at(R_CAT, TILES, D)
        wsT = cat[:, 0:2, 0:AW].rearrange("p a (g q) -> p a g q", q=P)
        pre = [cat[:, 2, 0:AW], cat[:, 3, 0:AW]]
        vn = at(R_VN, TILES, AW)
        relT = at(R_LOW, 2, BIAS_W)
        scored = at(R_LOW + 3840, 2, L_SAMPLE)
        probs = at(R_LOW + 5888, 3, L_SAMPLE)
        probsT = at(R_LOW + 8960, 2, KT, P)
        wout = at(R_WOUT, KT, D)
        ln1_g, ln1_b = at(R_VN, D), at(R_VN + 1024, D)
        wr = at(R_VN + 2048, KT, EXPERTS)
        x_again = at(R_VN + 2176, 2, D)
        resid = at(R_QKV, 2, D)
        x1 = at(R_QKV + 2048, 2, D)
        ax1 = at(R_QKV + 4096, 2, D)
        catT = at(R_QKV + 6144, 2, KT, P)
        x1T = at(R_QKV + 8192, 2, KT, P)
        aff_a = at(30720, L_SAMPLE)
        aff_b = at(31744, L_SAMPLE)
        o = 32768
        top_val, top_idx, top_idf = at(o, CAP_S), at(o + 128, CAP_S).bitcast(U32), at(o + 256, CAP_S)
        aff = at(o + 384, 2, EXPERTS)
        aff_e = at(o + 416, 2, EXPERTS)
        gates = at(o + 448, 2, EXPERTS + 1)
        idx = at(o + 482, 2, EXPERTS + 1).bitcast(U32)
        idx_g = at(o + 516, 2).bitcast(U32)
        idx_s = at(o + 518, 2).bitcast(U32)
        smx, ssum = at(o + 520, 2), at(o + 522, 2)
        o = R_WOUT + 2 * SPLIT * UW
        xs = at(o, D)
        xs_p = at(o + 1024, D)
        b0 = o + 2048 - 11264 - 2 * SPLIT * UW
        hid, sg = (between[:, b:b + 4 * SLOTS].rearrange("p (r j s) -> p r j s", r=2, j=2) for b in (b0, b0 + 4 * SLOTS))
        b0 = o + 6656 - 11264 - 2 * SPLIT * UW
        gate_sum = between[:, b0:b0 + 4 * SLOTS].rearrange("p (r j s) -> p r j s", r=2, j=2)
        up_sum = between[:, b0 + 4 * SLOTS:b0 + 6 * SLOTS].rearrange("p (j s) -> p j s", j=2)
        yT = at(o + 3328, KT, SLOTS)
        ys = at(o + 4608, D)
        ys_p = at(o + 5632, D)
        ln2_g, ln2_b = at(R_VN, D), at(R_VN + 1024, D)
        fin_in = at(R_CAT, 5, D)
        fin_out = at(R_CAT + 5120, 5, D)
        o = R_SMALL
        rowb = at(o, 3, AW)
        gln_g, gln_b = at(o + 1536, AW), at(o + 2048, AW)
        ident = at(o + 2560, P)
        o += 2688
        table = at(o, HEADS)
        b_qk = at(o + 8, 8)
        b_s = at(o + 16, 8)
        half_neg = at(o + 24, 1)
        rstd = at(o + 25, TILES)
        veps = at(o + 35, 1)
        mv = at(o + 36, TILES, 2)
        stats = at(o + 56, 2, 6)
        mx = at(o + 68, 4)
        nmx = at(o + 72, 4)
        den = at(o + 76, 8)
        rden = at(o + 84, 2)
        lmx = at(o + 86, 1)

        s_const, s_rel_in, s_bs, s_rows = sem("const_in"), sem("rel_in"), sem("small_in"), sem("rows_in")
        s_x = [sem(f"x_in{t}") for t in range(TILES)]
        s_win = [sem(f"win_in{i}") for i in range(2)]
        s_ident, s_table1 = sem("ident_ready"), sem("table_one")
        s_job = sem("job_done")
        s_free = {"act": sem("freed_by_act"), "dve": sem("freed_by_dve")}
        s_rel_out, s_relT = sem("rel_stored"), [sem(f"relT_in{i}") for i in range(2)]
        s_gelu = sem("gelu_done")
        s_stat, s_rstd, s_vn = sem("stats_done"), sem("rstd_ready"), sem("vn_ready")
        s_pool = sem("pool_chain")
        s_dch = sem("dve_chain")
        s_bq = sem("bq_scaled")
        s_qk, s_scored, s_probs = sem("qk_done"), sem("scored"), sem("probs_ready")
        s_pt, s_ptc, s_pv, s_att = sem("probsT_done"), sem("probsT_copied"), sem("pv_done"), sem("att_out")
        s_wout, s_ln1, s_xa = sem("wout_in"), sem("ln1_in"), [sem(f"x_again{i}") for i in range(2)]
        s_catT, s_catTc, s_mix = sem("catT_done"), sem("catT_copied"), sem("mix_done")
        s_res = sem("resid_done")
        s_x1, s_ax1, s_x1st = sem("x1_ready"), sem("ax1_ready"), [sem(f"x1_stored{i}") for i in range(2)]
        s_x1T, s_x1Tc, s_log = sem("x1T_done"), sem("x1T_copied"), sem("logits_done")
        s_smx, s_sexp, s_aff, s_affT, s_affTc = (sem("logit_max"), sem("logit_exp"), sem("aff_ready"),
                                                 sem("affT_done"), sem("affT_copied"))
        s_top, s_topT, s_idx = sem("top_ready"), sem("topT_done"), sem("idx_ready")
        s_unit_in = [sem(f"unit_in{i}") for i in range(RING)]
        s_unit = sem("units_done")
        s_hi, s_lo = sem("unit_high"), sem("unit_low")
        s_gate, s_up = sem("gate_summed"), sem("up_summed")
        s_silu, s_mul, s_hh, s_hid = sem("silu_done"), sem("hidden_done"), sem("hidden_high"), sem("hidden_low")
        s_gath = sem("gathered")
        s_xsT, s_xsH, s_xsL = sem("xsT_done"), sem("xs_high"), sem("xs_low")
        s_yT, s_yt, s_ys = sem("yT_copied"), sem("y_transposed"), sem("ys_ready")
        s_scat, s_gi0, s_gi, s_si = sem("scattered"), sem("first_idx"), sem("gather_idx"), sem("scatter_idx")
        s_fin_in = [sem(f"fin_in{i}") for i in range(5)]
        s_ln2, s_fin, s_out = sem("ln2_in"), sem("fin_ready"), [sem(f"out_stored{i}") for i in range(5)]

        jobs = [("rel", i, "dve") for i in range(4)] + [("ws", i, "act") for i in range(2)]
        jobs += [("xT", (t, i), "act" if i else "dve") for t in range(TILES) for i in range(2)]
        jobs += [("gv", t, "dve") for t in range(TILES)] + [("gu", t, "dve") for t in range(TILES)]
        CH = [(0, 512), (512, 512), (1024, 256)]
        jobs += [("k", (et, c), "act") for et in range(4) for c in range(3)]
        jobs += [("gm", t, "dve") for t in range(TILES)]
        jobs += [("q", (et, c), "act") for et in range(4) for c in range(3)]
        jobs += [("v", t, "dve") for t in range(TILES)]
        freed = []
        for n, (_, _, eng) in enumerate(jobs):
            freed.append(1 + sum(e == eng for _, _, e in jobs[:n]))
        BLOCKS = [("gv", 4 * AW), ("gu", 3 * AW), ("k", AW), ("q", 0), ("v", 2 * AW)]
        block_end = [1 + max(n for n, j in enumerate(jobs) if j[0] == name) for name, _ in BLOCKS]

        units = [(h, g, qt) for h in range(HEADS) for g in range(2)
                 for qt in range(PT if g == 0 else TILES - PT)]
        NU = len(units)
        glen = (L_PROMPT, L_SAMPLE)
        gtile = (0, PT)

        block = ctx.enter_context(nc.Block())

        def unit_src(e, u):
            if u < GU_UNITS:
                pr, kind = u // 4, u % 4
                w = (w_gate, w_up)[kind // 2]
                k0 = (kind % 2) * (KT // 2) * P
                return w[e, k0:k0 + KT // 2 * P, pr * 2 * P:(pr + 1) * 2 * P].rearrange("(k p) f -> p k f", p=P)
            half, pr = divmod(u - GU_UNITS, DN_UNITS)
            return w_down[e, pr * 2 * P:(pr + 1) * 2 * P, half * 512:(half + 1) * 512].rearrange("(k p) f -> p k f", p=P)

        def unit_dst(u):
            k = KT // 2 if u % UNITS < GU_UNITS else 2
            return raw[:, u % RING, :].rearrange("p (k f) -> p k f", k=k)

        @block.sync
        def _(sp):
            def load_block(b):
                if b >= 2:
                    sp.wait_ge(s_job, block_end[b - 2])
                c = BLOCKS[b][1]
                sp.dma_start(win[:, b % 2], w_in[:, c:c + AW].rearrange("(k p) f -> p k f", p=P)).then_inc(s_win[b % 2], 16)

            for t in range(TILES):
                sp.dma_start(x_rows[:, t], token_rows(a["x_prompt"], a["x_sample"], t)).then_inc(s_x[t], 16)
                if t in (3, 7):
                    load_block(t // 4)
            sp.wait_ge(s_free["dve"], 4)
            sp.dma_start(rel_d[:, :], rel_bias[0:HEADS, :]).then_inc(s_rel_out, 16)
            for b in range(2, 5):
                load_block(b)
            sp.wait_ge(s_job, len(jobs))
            sp.wait_ge(s_rel_out, 16)

            def load_relT(h):
                if h >= 2:
                    sp.wait_ge(s_scored, 10 * (h - 1))
                src = bass.AP(tensor=rel_d.tensor, offset=h * REL, ap=[[1, P], [1, BIAS_W]])
                sp.dma_start(relT[:, h % 2, :], src).then_inc(s_relT[h % 2], 16)

            load_relT(0)
            load_relT(1)
            sp.dma_start(wout[:, :, :], w_out.rearrange("(k p) f -> p k f", p=P)).then_inc(s_wout, 16)
            for dst, name in ((ln1_g, "ln1_g"), (ln1_b, "ln1_b")):
                sp.dma_start(dst, a[name][0:1, :].to_broadcast([P, D])).then_inc(s_ln1, 16)
            sp.dma_start(wr, a["w_router"][0].rearrange("(k p) e -> p k e", p=P)).then_inc(s_ln1, 16)

            def load_x(t):
                if t >= 2:
                    sp.wait_ge(s_res, t - 1)
                sp.dma_start(x_again[:, t % 2], token_rows(a["x_prompt"], a["x_sample"], t)).then_inc(s_xa[t % 2], 16)

            load_x(0)
            load_x(1)
            for h in range(2, HEADS):
                load_relT(h)
            sp.wait_ge(s_pv, NU)
            for u in range(RING):
                sp.dma_start(unit_dst(u), unit_src(0, u)).then_inc(s_unit_in[u], 16)
            for t in range(TILES):
                if t + 2 < TILES:
                    load_x(t + 2)
                sp.wait_ge(s_x1, t + 1)
                sp.dma_start(x1_d[t * P:(t + 1) * P, :], x1[:, t % 2]).then_inc(s_x1st[t % 2], 16)
                sp.wait_ge(s_ax1, t + 1)
                sp.dma_start(acc_d[t * P:(t + 1) * P, :], ax1[:, t % 2]).then_inc(s_x1st[t % 2], 16)
            for dst, name in ((ln2_g, "ln2_g"), (ln2_b, "ln2_b")):
                sp.dma_start(dst, a[name][0:1, :].to_broadcast([P, D])).then_inc(s_ln2, 16)

            with sp.Fori(0, EXPERTS - 1) as e:
                for u in range(UNITS):
                    n = u + RING
                    if n % UNITS not in (0, 2, GU_UNITS):
                        sp.wait_ge(s_lo, e * UNITS + (u + 1 + ((n + 1) % UNITS in (0, 2, GU_UNITS))))
                    sp.dma_start(unit_dst(n), unit_src(e + n // UNITS, n % UNITS)).then_inc(s_unit_in[n % RING], 16)
            for u in range(UNITS - RING):
                n = u + RING
                sp.wait_ge(s_lo, (EXPERTS - 1) * UNITS + u + 1)
                sp.dma_start(unit_dst(n), unit_src(EXPERTS - 1, n)).then_inc(s_unit_in[n % RING], 16)

            sp.wait_ge(s_scat, 32 * EXPERTS)
            for t in range(TILES + 3):
                if t < TILES:
                    if t >= 5:
                        sp.wait_ge(s_fin, t - 4)
                    sp.dma_start(fin_in[:, t % 5], acc_d[t * P:(t + 1) * P, :]).then_inc(s_fin_in[t % 5], 16)
                if t >= 3:
                    sp.wait_ge(s_fin, t - 2)
                    sp.dma_start(token_rows(out_prompt, out_sample, t - 3), fin_out[:, (t - 3) % 5]).then_inc(s_out[(t - 3) % 5], 16)
            for i in range(5):
                sp.wait_ge(s_out[i], 16 * (TILES // 5))

        @block.tensor
        def _(pe):
            pe.wait_ge(s_ident, 2)
            jn = [0]
            waited = {"act": 0, "dve": 0}

            def job(name):
                n = jn[0]
                assert jobs[n][0] == name
                if n >= 8:
                    eng, c = jobs[n - 8][2], freed[n - 8]
                    if c > waited[eng]:
                        pe.wait_ge(s_free[eng], c)
                        waited[eng] = c
                jn[0] += 1
                return psum[:, n % 8, :], jobs[n][1]

            pe.wait_ge(s_rel_in, 32)
            pe.wait_ge(s_table1, 1)
            for i in range(4):
                bank, _ = job("rel")
                nc.tensor.matmul(bank[0:HEADS, :], table[0:N_BUCKETS + 1, :], rel_rows[0:N_BUCKETS + 1, i * 512:(i + 1) * 512],
                                 start=True, stop=True).then_inc(s_job, 1)
            pe.wait_ge(s_rows, 16)
            for i in range(2):
                bank, _ = job("ws")
                for g in range(4):
                    last = nc.tensor.transpose(bank[:, g * P:(g + 1) * P], ws_rows[:, 4 * i + g, :], ident)
                last.then_inc(s_job, 1)
            for t in range(TILES):
                pe.wait_ge(s_x[t], 16)
                for i in range(2):
                    bank, _ = job("xT")
                    for k in range(4):
                        last = nc.tensor.transpose(bank[:, k * P:(k + 1) * P], x_rows[:, t, (4 * i + k) * P:(4 * i + k + 1) * P], ident)
                    last.then_inc(s_job, 1)
            nx = 6 + 2 * TILES
            pe.wait_ge(s_free["dve"], freed[nx - 2])
            pe.wait_ge(s_free["act"], freed[nx - 1])
            for b, (name, _) in enumerate(BLOCKS):
                if name == "q":
                    for t in range(TILES):
                        bank, _ = job("gm")
                        pe.wait_ge(s_vn, t + 1)
                        for g in range(8):
                            last = nc.tensor.matmul(bank[:, g * HD:(g + 1) * HD], wsT[:, g // 4, g % 4, :],
                                                    vn[:, t, g * HD:(g + 1) * HD], start=True, stop=True)
                        last.then_inc(s_job, 1)
                pe.wait_ge(s_win[b % 2], 16 * (b // 2 + 1))
                w = win[:, b % 2]
                if name in ("q", "k"):
                    for et in range(4):
                        for c0, cn in CH:
                            bank, _ = job(name)
                            for k in range(KT):
                                last = nc.tensor.matmul(bank[:, 0:cn], w[:, k, et * P:(et + 1) * P], xT[:, k, c0:c0 + cn],
                                                        start=k == 0, stop=k == KT - 1)
                            last.then_inc(s_job, 1)
                else:
                    for t in range(TILES):
                        bank, _ = job(name)
                        for k in range(KT):
                            last = nc.tensor.matmul(bank, xT[:, k, t * P:(t + 1) * P], w[:, k, :],
                                                    start=k == 0, stop=k == KT - 1)
                        last.then_inc(s_job, 1)

            for eng in ("act", "dve"):
                pe.wait_ge(s_free[eng], sum(e == eng for _, _, e in jobs))
            for n in range(NU + 3):
                if n < NU:
                    h, g, qt = units[n]
                    if n >= 2:
                        pe.wait_ge(s_scored, n - 1)
                    base, t0 = HD * (h % 2), gtile[g] * P
                    q = qT[base:base + HD, h // 2, t0 + qt * P:t0 + (qt + 1) * P]
                    for c in range(0, glen[g], 512):
                        cn = min(512, glen[g])
                        last = nc.tensor.matmul(psum[:, 2 * (n % 2) + c // 512, 0:cn], q,
                                                kT[base:base + HD, h // 2, t0 + c:t0 + c + cn], start=True, stop=True)
                    last.then_inc(s_qk, 1)
                if 0 <= n - 2 < NU:
                    m = n - 2
                    pe.wait_ge(s_probs, m + 1)
                    if m >= 1:
                        pe.wait_ge(s_ptc, m)
                    for kt in range(glen[units[m][1]] // P):
                        last = nc.tensor.transpose(psum[:, 4 + kt // 4, kt % 4 * P:(kt % 4 + 1) * P],
                                                   probs[:, m % 3, kt * P:(kt + 1) * P], ident)
                    last.then_inc(s_pt, 1)
                if 0 <= n - 3 < NU:
                    m = n - 3
                    h, g, qt = units[m]
                    pe.wait_ge(s_ptc, m + 1)
                    if m >= 2:
                        pe.wait_ge(s_att, m - 1)
                    nk = glen[g] // P
                    for kt in range(nk):
                        last = nc.tensor.matmul(psum[:, 6 + m % 2, 0:HD], probsT[:, m % 2, kt, :],
                                                v_rows[:, gtile[g] + kt, h * HD:(h + 1) * HD],
                                                start=kt == 0, stop=kt == nk - 1)
                    last.then_inc(s_pv, 1)

            pe.wait_ge(s_att, NU)
            pe.wait_ge(s_wout, 16)
            pe.wait_ge(s_ln1, 48)

            def cat_transposes(t):
                if t >= 1:
                    pe.wait_ge(s_catTc, t)
                for k in range(KT):
                    last = nc.tensor.transpose(psum[:, k // 4, k % 4 * P:(k % 4 + 1) * P], cat[:, t, k * P:(k + 1) * P], ident)
                last.then_inc(s_catT, 1)

            def mix(t, j):
                if j == 0:
                    pe.wait_ge(s_catTc, t + 1)
                    if t >= 2:
                        pe.wait_ge(s_res, t - 1)
                for k in range(KT):
                    last = nc.tensor.matmul(psum[:, 2 + 2 * (t % 2) + j, :], catT[:, t % 2, k, :], wout[:, k, j * 512:(j + 1) * 512],
                                            start=k == 0, stop=k == KT - 1)
                if j == 1:
                    last.then_inc(s_mix, 1)

            def x1_transposes(t):
                pe.wait_ge(s_x1, t + 1)
                if t >= 1:
                    pe.wait_ge(s_smx, t)
                    pe.wait_ge(s_sexp, t)
                    pe.wait_ge(s_affTc, t)
                for k in range(KT):
                    last = nc.tensor.transpose(psum[:, 6 + k // 4, k % 4 * P:(k % 4 + 1) * P], x1[:, t % 2, k * P:(k + 1) * P], ident)
                last.then_inc(s_x1T, 1)

            def logits(t):
                pe.wait_ge(s_x1Tc, t + 1)
                for k in range(KT):
                    last = nc.tensor.matmul(psum[:, 6, 0:EXPERTS], x1T[:, t % 2, k, :], wr[:, k, :], start=k == 0, stop=k == KT - 1)
                last.then_inc(s_log, 1)

            def aff_transpose(t):
                pe.wait_ge(s_aff, t + 1)
                if t >= 1:
                    pe.wait_ge(s_affTc, t)
                nc.tensor.transpose(psum[0:EXPERTS, 7, 0:P], aff[:, t % 2, :], ident).then_inc(s_affT, 1)

            cat_transposes(0)
            for t in range(TILES + 1):
                if t < TILES:
                    mix(t, 0)
                if t >= 2:
                    aff_transpose(t - 2)
                if t >= 1:
                    x1_transposes(t - 1)
                if t + 1 < TILES:
                    cat_transposes(t + 1)
                if t < TILES:
                    mix(t, 1)
                if t >= 1:
                    logits(t - 1)
            aff_transpose(TILES - 1)

            pe.wait_ge(s_top, 1)
            nc.tensor.transpose(psum[:, 0, 0:48], top_val[0:48, :], ident[0:48, 0:48])
            nc.tensor.transpose(psum[:, 1, 0:48], top_idf[0:48, :], ident[0:48, 0:48]).then_inc(s_topT, 1)

            def xs_transposes():
                for k in range(KT):
                    o0 = k % 3 * SLOTS
                    nc.tensor.transpose(psum[:, k // 3, o0:o0 + CAP_S], xs[:, k * P:(k + 1) * P], ident)
                    last = nc.tensor.transpose(psum[:, k // 3, o0 + CAP_S:o0 + SLOTS], xs_p[0:CAP_P, k * P:(k + 1) * P],
                                               ident[0:CAP_P, 0:CAP_P])
                last.then_inc(s_xsT, 1)

            def y_transposes(half, bank_s, bank_p):
                for i in range(4):
                    nc.tensor.transpose(psum[:, bank_s, i * P:(i + 1) * P], yT[:, 4 * half + i, 0:CAP_S], ident)
                    last = nc.tensor.transpose(psum[0:CAP_P, bank_p, i * P:(i + 1) * P], yT[:, 4 * half + i, CAP_S:SLOTS], ident)
                last.then_inc(s_yt, 1)

            pe.wait_ge(s_idx, 1)
            pe.wait_ge(s_gath, 32)
            xs_transposes()
            def product(bank, u, cols, moving, first, last_one):
                nc.tensor.matmul(bank[:, 0:2 * SLOTS], w_parts[:, HI, u % SPLIT, cols], moving(slice(HI, LO + 1)),
                                 start=first, stop=False)
                return nc.tensor.matmul(bank[:, 0:SLOTS], w_parts[:, LO, u % SPLIT, cols], moving(HI), start=False, stop=last_one)

            pe.sem_inc(s_unit, SPLIT)
            with pe.Fori(0, EXPERTS) as e:
                pe.wait_ge(s_xsL, e + 1)
                pe.wait_ge(s_ys, e * 2 + 1)
                for pr in range(PAIRS):
                    for kind in range(4):
                        u = 4 * pr + kind
                        pe.wait_ge(s_lo, e * UNITS + (u + 1))
                        if kind == 0:
                            pe.wait_ge(s_gate, e * PAIRS + (pr + 1))
                        if kind == 2:
                            pe.wait_ge(s_mul, e * PAIRS + (pr + 1))
                        for j in range(2):
                            for k in range(KT // 2):
                                kk = kind % 2 * (KT // 2) + k
                                last = product(psum[:, 2 * (kind // 2) + j, :], u, slice((2 * k + j) * P, (2 * k + j + 1) * P),
                                               lambda part, kk=kk: xs_parts[:, part, kk, :], kk == 0, kk == KT - 1)
                        last.then_inc(s_unit, 1)
                    if pr == 1:
                        pe.wait_ge(s_yT, e * 8 + 4)
                        y_transposes(1, 4, 5)
                for half in range(2):
                    for pr in range(PAIRS):
                        u = GU_UNITS + DN_UNITS * half + pr
                        pe.wait_ge(s_lo, e * UNITS + (u + 1))
                        if half == 0:
                            pe.wait_ge(s_hid, e * PAIRS + (pr + 2))
                            if pr == 0:
                                pe.wait_ge(s_ys, e * 2 + 2)
                        order = [(j, i) for j in range(2) for i in range(4)] if pr < PAIRS - 1 else \
                                [(j, i) for i in range(4) for j in range(2)]
                        for j, i in order:
                            if pr == 0 and half == 1 and j == 0:
                                pe.wait_ge(s_yT, e * 8 + (5 + i))
                            last = product(psum[:, 4 + i, :], u, slice((4 * j + i) * P, (4 * j + i + 1) * P),
                                           lambda part, f=2 * pr + j: h_parts[:, part, f, :],
                                           pr == 0 and j == 0, pr == PAIRS - 1 and j == 1)
                        last.then_inc(s_unit, 1)
                        if half == 0 and pr == 1:
                            pe.wait_ge(s_mul, e * PAIRS + (PAIRS + 1))
                            pe.wait_ge(s_gath, e * 32 + 64)
                            xs_transposes()
                        if half == 1 and pr == 2:
                            pe.wait_ge(s_xsL, e + 2)
                            pe.wait_ge(s_yT, e * 8 + 8)
                            y_transposes(0, 3, 0)
            pe.wait_ge(s_yT, EXPERTS * 8 + 4)
            pe.wait_ge(s_ys, EXPERTS * 2 + 1)
            y_transposes(1, 4, 5)

        @block.scalar
        def _(act):
            act.dma_start(rel_rows[0:N_BUCKETS + 1, :], a["rel_rows"]).then_inc(s_rel_in, 16)
            act.dma_start(table[0:N_BUCKETS, :], a["rel_bias_table"]).then_inc(s_rel_in, 16)
            act.dma_start(ws_rows, a["gmlp_w_s"][0].rearrange("g p q -> p g q")).then_inc(s_rows, 16)
            act.dma_start(rowb, a["b_in"][0:1, 2 * AW:5 * AW].to_broadcast([P, 3 * AW])
                          .rearrange("p (a b) -> p a b", a=3)).then_inc(s_const, 16)
            act.dma_start(gln_g, a["gmlp_ln_g"][0:1, :].to_broadcast([P, AW])).then_inc(s_const, 16)
            act.dma_start(gln_b, a["gmlp_ln_b"][0:1, :].to_broadcast([P, AW])).then_inc(s_const, 16)
            act.dma_start(b_qk, a["b_in"][0, 0:2 * AW].rearrange("(e p) -> p e", p=P),
                          allow_slow_non_contiguous=True).then_inc(s_bs, 16)
            act.dma_start(b_s, a["gmlp_b_s"][0].rearrange("g p -> p g"),
                          allow_slow_non_contiguous=True).then_inc(s_bs, 16)
            act.wait_ge(s_bs, 32)
            nc.scalar.mul(b_qk[:, 0:4], b_qk[:, 0:4], HD ** -0.5).then_inc(s_bq, 1)
            gel = 0
            for n, (name, arg, eng) in enumerate(jobs):
                if name in ("gv", "gu"):
                    act.wait_ge(s_free["dve"], freed[n])
                    dst = vn[:, arg, :] if name == "gv" else cat[:, arg, AW:2 * AW]
                    nc.scalar.activation(dst, pre[gel % 2], ACT.Gelu_apprx_tanh).then_inc(s_gelu, 1)
                    gel += 1
                if eng != "act":
                    continue
                act.wait_ge(s_job, n + 1)
                bank = psum[:, n % 8, :]
                if name == "ws":
                    nc.scalar.copy(wsT[:, arg], bank.rearrange("p (g q) -> p g q", q=P)).then_inc(s_free["act"], 1)
                elif name == "xT":
                    t, i = arg
                    nc.scalar.copy(xT[:, 4 * i:4 * i + 4, t * P:(t + 1) * P], bank.rearrange("p (k c) -> p k c", k=4)).then_inc(s_free["act"], 1)
                else:
                    et, c = arg
                    c0, cn = CH[c]
                    if name == "q" and arg == (0, 0):
                        act.wait_ge(s_bq, 1)
                    dst = (qT if name == "q" else kT)[:, et, c0:c0 + cn]
                    b = b_qk[:, et:et + 1] if name == "q" else b_qk[:, 4 + et:5 + et]
                    nc.scalar.activation(dst, bank[:, 0:cn], ACT.Identity, bias=b,
                                         scale=HD ** -0.5 if name == "q" else 1.0).then_inc(s_free["act"], 1)

            for n in range(NU + 2):
                if n >= 2:
                    m = n - 2
                    act.wait_ge(s_pt, m + 1)
                    if m >= 2:
                        act.wait_ge(s_pv, m - 1)
                    nk = glen[units[m][1]] // P
                    src = psum[:, 4:6, :].rearrange("p b (k c) -> p (b k) c", c=P)[:, 0:nk, :]
                    nc.scalar.copy(probsT[:, m % 2, 0:nk, :], src).then_inc(s_ptc, 1)
                if n < NU:
                    L = glen[units[n][1]]
                    act.wait_ge(s_scored, n + 1)
                    if n >= 3:
                        act.wait_ge(s_pt, n - 2)
                    nc.scalar.activation(probs[:, n % 3, 0:L], scored[:, n % 2, 0:L], ACT.Exp, bias=nmx[:, n % 4:n % 4 + 1],
                                         scale=1.0, accum_out=den[:, n % 8:n % 8 + 1]).then_inc(s_probs, 1)

            def cat_copy(t):
                act.wait_ge(s_catT, t + 1)
                if t >= 2:
                    act.wait_ge(s_mix, t - 1)
                nc.scalar.copy(catT[:, t % 2], psum[:, 0:2, :].rearrange("p b (k c) -> p (b k) c", c=P)).then_inc(s_catTc, 1)

            cat_copy(0)
            for t in range(TILES + 1):
                if t >= 1:
                    m = t - 1
                    act.wait_ge(s_x1, m + 1)
                    if m >= 2:
                        act.wait_ge(s_x1st[m % 2], 32 * (m // 2))
                    nc.scalar.mul(ax1[:, m % 2], x1[:, m % 2], ALPHA).then_inc(s_ax1, 1)
                    act.wait_ge(s_x1T, m + 1)
                    if m >= 2:
                        act.wait_ge(s_log, m - 1)
                    nc.scalar.copy(x1T[:, m % 2], psum[:, 6:8, :].rearrange("p b (k c) -> p (b k) c", c=P)).then_inc(s_x1Tc, 1)
                if t + 1 < TILES:
                    cat_copy(t + 1)
                if t >= 1:
                    m = t - 1
                    act.wait_ge(s_smx, m + 1)
                    if m >= 2:
                        act.wait_ge(s_aff, m - 1)
                    nc.scalar.activation(aff_e[:, m % 2], psum[:, 6, 0:EXPERTS], ACT.Exp, bias=smx[:, m % 2:m % 2 + 1], scale=1.0,
                                         accum_out=ssum[:, m % 2:m % 2 + 1]).then_inc(s_sexp, 1)

            def xs_copy(e_done):
                act.wait_ge(s_xsT, e_done)
                for b in range(3):
                    nk = min(3, KT - 3 * b)
                    last = nc.scalar.copy(xs_parts[:, HI, 3 * b:3 * b + nk, :], psum[:, b, 0:nk * SLOTS].rearrange("p (k c) -> p k c", k=nk))
                last.then_inc(s_xsH, 1)

            def ys_copy(half, bank_s, bank_p, gate_s, gate_p):
                c = slice(512 * half, 512 * half + 512)
                nc.scalar.activation(ys[:, c], psum[:, bank_s, :], ACT.Copy, scale=gate_s)
                nc.scalar.activation(ys_p[0:CAP_P, c], psum[0:CAP_P, bank_p, :], ACT.Copy, scale=gate_p).then_inc(s_ys, 1)

            act.wait_ge(s_idx, 1)
            xs_copy(1)
            act.sem_inc(s_silu, 1)
            act.sem_inc(s_ys, 1)
            with act.Fori(0, EXPERTS) as e:
                for u in range(UNITS):
                    act.wait_ge(s_unit_in[u % RING], e * (16 * UNITS // RING) + 16 * (u // RING + 1))
                    act.wait_ge(s_unit, e * UNITS + (u + 1))
                    nc.scalar.copy(w_parts[:, HI, u % SPLIT, :], raw[:, u % RING, :]).then_inc(s_hi, 1)
                    if u % 4 == 3 and 7 <= u <= GU_UNITS + 3:
                        pr = (u - 7) // 4
                        act.wait_ge(s_gate, e * PAIRS + (pr + 2))
                        act.wait_ge(s_mul, e * PAIRS + max(pr, 1))
                        nc.scalar.activation(sg[:, pr % 2], gate_sum[:, pr % 2], ACT.Silu).then_inc(s_silu, 1)
                    if u % 4 == 1 and 9 <= u <= GU_UNITS + 5:
                        pr = (u - 9) // 4
                        act.wait_ge(s_mul, e * PAIRS + (pr + 2))
                        nc.scalar.copy(h_parts[:, HI, 2 * pr:2 * pr + 2, :], hid[:, pr % 2]).then_inc(s_hh, 1)
                    if u == 13:
                        act.wait_ge(s_yt, e * 2 + 1)
                        ys_copy(1, 4, 5, gates[:, 0, bass.ds(e, 1)], gates[0:CAP_P, 1, bass.ds(e, 1)])
                    if u == GU_UNITS + 7:
                        xs_copy(e + 2)
                    if u == GU_UNITS + DN_UNITS + 8:
                        act.wait_ge(s_yt, e * 2 + 2)
                        act.wait_ge(s_gi, e + 1)
                        ys_copy(0, 3, 0, gates[:, 0, bass.ds(e + 1, 1)], gates[0:CAP_P, 1, bass.ds(e + 1, 1)])
            act.wait_ge(s_yt, EXPERTS * 2 + 1)
            ys_copy(1, 4, 5, gates[:, 0, EXPERTS:EXPERTS + 1], gates[0:CAP_P, 1, EXPERTS:EXPERTS + 1])

        @block.vector
        def _(dve):
            chain = [0]

            def link(ins):
                chain[0] += 1
                ins.then_inc(s_dch, 1)
                dve.wait_ge(s_dch, chain[0])

            nc.vector.memset(table[N_BUCKETS:N_BUCKETS + 1, :], 1.0).then_inc(s_table1, 1)

            def gmlp_stats(t):
                dve.wait_ge(s_gelu, t + 1)
                if t:
                    dve.wait_ge(s_stat, t)
                link(nc.vector.bn_stats(stats[:, 0, :], vn[:, t, :]))
                nc.vector.bn_aggr(mv[:, t, :], stats[:, 0, :]).then_inc(s_stat, 1)

            def gmlp_norm(t):
                dve.wait_ge(s_rstd, t + 1)
                link(nc.vector.scalar_tensor_tensor(vn[:, t, :], vn[:, t, :], mv[:, t, 0:1], gln_g, ALU.subtract, ALU.mult))
                nc.vector.scalar_tensor_tensor(vn[:, t, :], vn[:, t, :], rstd[:, t:t + 1], gln_b, ALU.mult, ALU.add).then_inc(s_vn, 1)

            nat = 0
            for n, (name, arg, eng) in enumerate(jobs):
                if eng != "dve":
                    continue
                dve.wait_ge(s_job, n + 1)
                bank = psum[:, n % 8, :]
                done = lambda ins: ins.then_inc(s_free["dve"], 1)
                if name == "rel":
                    done(nc.vector.tensor_copy(rel_bias[0:HEADS, arg * 512:(arg + 1) * 512], bank[0:HEADS, :]))
                elif name == "xT":
                    t, i = arg
                    done(nc.vector.tensor_copy(xT[:, 4 * i:4 * i + 4, t * P:(t + 1) * P], bank.rearrange("p (k c) -> p k c", k=4)))
                elif name in ("gv", "gu"):
                    if nat == 0:
                        dve.wait_ge(s_const, 48)
                    if nat >= 2:
                        dve.wait_ge(s_gelu, nat - 1)
                    done(nc.vector.tensor_tensor(pre[nat % 2], bank, rowb[:, 2 if name == "gv" else 1, :], ALU.add))
                    if 1 <= nat <= TILES:
                        gmlp_stats(nat - 1)
                    if 2 <= nat <= TILES + 1:
                        gmlp_norm(nat - 2)
                    nat += 1
                elif name == "gm":
                    if arg == 0:
                        dve.wait_ge(s_bs, 32)
                        dve.wait_ge(s_gelu, 2 * TILES)
                    g = vn[:, arg, :]
                    link(nc.vector.tensor_tensor(g.rearrange("p (g c) -> p g c", c=HD), bank.rearrange("p (g c) -> p g c", c=HD),
                                                 b_s.unsqueeze(2).to_broadcast([P, 8, HD]), ALU.add))
                    done(nc.vector.tensor_tensor(cat[:, arg, AW:2 * AW], cat[:, arg, AW:2 * AW], g, ALU.mult))
                elif name == "v":
                    if arg == 0:
                        dve.wait_ge(s_rel_out, 16)
                    done(nc.vector.tensor_tensor(v_rows[:, arg, :], bank, rowb[:, 0, :], ALU.add))

            for n in range(NU + 4):
                if n < NU:
                    h, g, qt = units[n]
                    L = glen[g]
                    dve.wait_ge(s_qk, n + 1)
                    if n >= 2:
                        dve.wait_ge(s_probs, n - 1)
                    if g == 0 and qt == 0:
                        dve.wait_ge(s_relT[h % 2], 16 * (h // 2 + 1))
                    hi = qt * P + L_SAMPLE - 1
                    lo = hi - (L - 1)
                    bias = relT[:, h % 2, lo:hi + 1][:, ::-1]
                    src = psum[:, 2 * (n % 2):2 * (n % 2) + 2, :].rearrange("p b c -> p (b c)")[:, 0:L]
                    link(nc.vector.tensor_tensor_reduce(out=scored[:, n % 2, 0:L], in0=src, in1=bias, scale=1.0, scalar=-3e38,
                                                        op0=ALU.add, op1=ALU.max, accum_out=mx[:, n % 4:n % 4 + 1]))
                    nc.vector.tensor_scalar(nmx[:, n % 4:n % 4 + 1], mx[:, n % 4:n % 4 + 1], -1.0, None, ALU.mult).then_inc(s_scored, 1)
                if n >= 4:
                    m = n - 4
                    h, g, qt = units[m]
                    dve.wait_ge(s_pv, m + 1)
                    if m >= 2:
                        dve.wait_ge(s_att, m - 1)
                    link(nc.vector.reciprocal(rden[:, m % 2:m % 2 + 1], den[:, m % 8:m % 8 + 1]))
                    nc.vector.tensor_scalar(cat[:, gtile[g] + qt, h * HD:(h + 1) * HD], psum[:, 6 + m % 2, 0:HD],
                                            rden[:, m % 2:m % 2 + 1], None,
                                            ALU.mult).then_inc(s_att, 1)

            link(nc.vector.memset(aff_a[0:48, :], -1.0))

            def ln1(t):
                dve.wait_ge(s_mix, t + 1)
                dve.wait_ge(s_xa[t % 2], 16 * (t // 2 + 1))
                r = resid[:, t % 2]
                if t >= 2:
                    dve.wait_ge(s_x1, t - 1)
                link_res(nc.vector.scalar_tensor_tensor(r, x_again[:, t % 2], ALPHA, psum[:, 2 + 2 * (t % 2):4 + 2 * (t % 2), :]
                                                        .rearrange("p b c -> p (b c)"), ALU.mult, ALU.add), t)
                dve.wait_ge(s_stat, TILES + t)
                for i in range(2):
                    ins = nc.vector.bn_stats(stats[:, i, :], r[:, i * 512:(i + 1) * 512])
                link(ins)
                nc.vector.bn_aggr(mv[:, t, :], stats).then_inc(s_stat, 1)
                dve.wait_ge(s_rstd, TILES + t + 1)
                link(nc.vector.scalar_tensor_tensor(r, r, mv[:, t, 0:1], ln1_g, ALU.subtract, ALU.mult))
                if t >= 2:
                    dve.wait_ge(s_x1st[t % 2], 32 * (t // 2))
                    dve.wait_ge(s_ax1, t - 1)
                    dve.wait_ge(s_x1T, t - 1)
                nc.vector.scalar_tensor_tensor(x1[:, t % 2], r, rstd[:, t:t + 1], ln1_b, ALU.mult, ALU.add).then_inc(s_x1, 1)

            def link_res(ins, t):
                ins.then_inc(s_res, 1)
                dve.wait_ge(s_res, t + 1)

            def soft_max(t):
                dve.wait_ge(s_log, t + 1)
                if t:
                    dve.wait_ge(s_smx, t)
                link(nc.vector.reduce_max(lmx, psum[:, 6, 0:EXPERTS], AX_X))
                nc.vector.tensor_scalar(smx[:, t % 2:t % 2 + 1], lmx, -1.0, None, ALU.mult).then_inc(s_smx, 1)

            def soft_norm(t):
                dve.wait_ge(s_sexp, t + 1)
                if t >= 2:
                    dve.wait_ge(s_affT, t - 1)
                dve.wait_ge(s_aff, t) if t else dve.wait_ge(s_att, NU)
                link(nc.vector.reciprocal(rden[:, 0:1], ssum[:, t % 2:t % 2 + 1]))
                nc.vector.tensor_scalar(aff[:, t % 2], aff_e[:, t % 2], rden[:, 0:1], None, ALU.mult).then_inc(s_aff, 1)

            def aff_copy(t):
                dve.wait_ge(s_affT, t + 1)
                dst = aff_a[32:32 + EXPERTS, t * P:(t + 1) * P] if t < PT else aff_a[0:EXPERTS, (t - PT) * P:(t - PT + 1) * P]
                nc.vector.tensor_copy(dst, psum[0:EXPERTS, 7, 0:P]).then_inc(s_affTc, 1)

            dve.wait_ge(s_ln1, 48)
            for t in range(TILES + 2):
                if 0 <= t - 2:
                    aff_copy(t - 2) if t - 2 < TILES - 1 else None
                if t < TILES:
                    ln1(t)
                if 0 <= t - 1 < TILES:
                    soft_max(t - 1)
                    soft_norm(t - 1)
            aff_copy(TILES - 1)

            dve.wait_ge(s_affTc, TILES)
            cur, nxt = aff_a, aff_b
            for i in range(CAP_S // 8):
                v8 = top_val[0:48, 8 * i:8 * i + 8]
                link(nc.vector.max(v8, cur[0:48, :]))
                nc.vector.max_index(top_idx[0:48, 8 * i:8 * i + 8], v8, cur[0:48, :])
                link(nc.vector.match_replace(nxt[0:48, :], v8, cur[0:48, :], -1.0))
                cur, nxt = nxt, cur
            link(nc.vector.tensor_copy(top_idf[0:48, :], top_idx[0:48, :]))
            nc.vector.tensor_scalar(top_idf[0:EXPERTS, :], top_idf[0:EXPERTS, :], float(L_PROMPT), None, ALU.add).then_inc(s_top, 1)
            link(nc.vector.memset(gates, 0.0))
            link(nc.vector.memset(yT, 0.0))
            dve.wait_ge(s_topT, 1)
            for g in range(2):
                c = slice(32 * g, 32 * g + EXPERTS)
                nc.vector.tensor_copy(gates[:, g, 1:EXPERTS + 1], psum[:, 0, c])
                nc.vector.tensor_copy(idx[:, g, 0:EXPERTS], psum[:, 1, c])
                ins = nc.vector.tensor_copy(idx[:, g, EXPERTS:EXPERTS + 1], psum[:, 1, c.stop - 1:c.stop])
            ins.then_inc(s_idx, 1)
            dve.wait_ge(s_idx, 1)


            def low(out, whole, high):
                return nc.vector.tensor_tensor(out, whole, high.bitcast(F32), ALU.subtract)

            def xs_low(count):
                dve.wait_ge(s_xsH, count)
                for b in range(3):
                    nk = min(3, KT - 3 * b)
                    ks = slice(3 * b, 3 * b + nk)
                    last = low(xs_parts[:, LO, ks, :], psum[:, b, 0:nk * SLOTS].rearrange("p (k c) -> p k c", k=nk), xs_parts[:, HI, ks, :])
                last.then_inc(s_xsL, 1)

            def both(out, banks):
                return nc.vector.reduce_sum(out, banks, AX_X)

            def y_copy(half, count):
                dve.wait_ge(s_unit, count)
                for i in range(4):
                    both(yT[:, 4 * half + i, :], psum[:, 4 + i, 0:2 * SLOTS].rearrange("p (c s) -> p s c", c=2)).then_inc(s_yT, 1)

            xs_low(1)
            dve.sem_inc(s_gate, 1)
            dve.sem_inc(s_mul, 1)
            dve.sem_inc(s_hid, 1)
            with dve.Fori(0, EXPERTS) as e:
                for u in range(UNITS):
                    dve.wait_ge(s_hi, e * UNITS + (u + 1))
                    low(w_parts[:, LO, u % SPLIT, :], raw[:, u % RING, :], w_parts[:, HI, u % SPLIT, :]).then_inc(s_lo, 1)
                    if u == 4:
                        y_copy(1, e * UNITS + SPLIT)
                    if u % 4 == 2 and 6 <= u <= GU_UNITS + 2:
                        pr = (u - 6) // 4
                        dve.wait_ge(s_unit, e * UNITS + (4 * pr + 2 + SPLIT))
                        dve.wait_ge(s_silu, e * PAIRS + max(pr, 1))
                        both(gate_sum[:, pr % 2], psum[:, 0:2, 0:2 * SLOTS].rearrange("p j (c s) -> p j s c", c=2)).then_inc(s_gate, 1)
                    if u % 4 == 0 and 8 <= u <= GU_UNITS + 4:
                        pr = (u - 8) // 4
                        dve.wait_ge(s_unit, e * UNITS + (4 * pr + 4 + SPLIT))
                        dve.wait_ge(s_mul, e * PAIRS + (pr + 1))
                        both(up_sum, psum[:, 2:4, 0:2 * SLOTS].rearrange("p j (c s) -> p j s c", c=2)).then_inc(s_up, 1)
                        dve.wait_ge(s_up, e * PAIRS + (pr + 1))
                        dve.wait_ge(s_silu, e * PAIRS + (pr + 2))
                        dve.wait_ge(s_hid, e * PAIRS + max(pr, 1))
                        nc.vector.tensor_tensor(hid[:, pr % 2], sg[:, pr % 2], up_sum, ALU.mult).then_inc(s_mul, 1)
                    if u % 4 == 2 and 10 <= u <= GU_UNITS + 6:
                        pr = (u - 10) // 4
                        dve.wait_ge(s_hh, e * PAIRS + (pr + 1))
                        low(h_parts[:, LO, 2 * pr:2 * pr + 2, :], hid[:, pr % 2], h_parts[:, HI, 2 * pr:2 * pr + 2, :]).then_inc(s_hid, 1)
                    if u == GU_UNITS + 8:
                        xs_low(e + 2)
                    if u == GU_UNITS + DN_UNITS + 4:
                        y_copy(0, e * UNITS + (GU_UNITS + DN_UNITS + SPLIT))
            y_copy(1, EXPERTS * UNITS + SPLIT)

            dve.wait_ge(s_ln2, 32)
            for t in range(TILES):
                dve.wait_ge(s_fin_in[t % 5], 16 * (t // 5 + 1))
                r = fin_in[:, t % 5]
                dve.wait_ge(s_stat, 2 * TILES + t)
                for i in range(2):
                    ins = nc.vector.bn_stats(stats[:, i, :], r[:, i * 512:(i + 1) * 512])
                link(ins)
                nc.vector.bn_aggr(mv[:, t, :], stats).then_inc(s_stat, 1)
                dve.wait_ge(s_rstd, 2 * TILES + t + 1)
                link(nc.vector.scalar_tensor_tensor(r, r, mv[:, t, 0:1], ln2_g, ALU.subtract, ALU.mult))
                if t >= 5:
                    dve.wait_ge(s_out[t % 5], 16 * (t // 5))
                nc.vector.scalar_tensor_tensor(fin_out[:, t % 5], r, rstd[:, t:t + 1], ln2_b, ALU.mult, ALU.add).then_inc(s_fin, 1)

        @block.gpsimd
        def _(pool):
            chain = [0]

            def link(ins):
                chain[0] += 1
                ins.then_inc(s_pool, 1)
                pool.wait_ge(s_pool, chain[0])

            nc.gpsimd.memset(ident, 0.0).then_inc(s_ident, 1)
            link(nc.gpsimd.memset(half_neg, -0.5))
            pool.wait_ge(s_ident, 1)
            nc.gpsimd.affine_select(out=ident, in_=ident, compare_op=ALU.not_equal, fill=1.0, base=0,
                                    pattern=[[-1, P]], channel_multiplier=1).then_inc(s_ident, 1)
            def rstds(lo, hi):
                for n in range(lo, hi):
                    t = n % TILES
                    pool.wait_ge(s_stat, n + 1)
                    if n:
                        pool.wait_ge(s_rstd, n)
                    link(nc.gpsimd.tensor_scalar(veps, mv[:, t, 1:2], EPS, None, ALU.add))
                    nc.gpsimd.tensor_tensor(rstd[:, t:t + 1], veps, half_neg, ALU.pow).then_inc(s_rstd, 1)

            rstds(0, 2 * TILES)

            def gather(e, copied, count):
                nc.gpsimd.tensor_copy(idx_g, idx[:, :, bass.ds(e, 1)].rearrange("p g o -> p (g o)")).then_inc(copied, 1)
                pool.wait_ge(s_idx, 1)
                pool.wait_ge(copied, count)
                pool.indirect_dma_start(xs, None, x1_d, bass.IndirectOffsetOnAxis(ap=idx_g[:, 0:1], axis=0)).then_inc(s_gath, 16)
                pool.indirect_dma_start(xs_p[0:CAP_P, :], None, x1_d,
                                        bass.IndirectOffsetOnAxis(ap=idx_g[0:CAP_P, 1:2], axis=0)).then_inc(s_gath, 16)

            for i in range(2):
                pool.wait_ge(s_x1st[i], 32 * (TILES // 2))
            pool.wait_ge(s_idx, 1)
            gather(0, s_gi0, 1)
            pool.wait_ge(s_xsT, 1)
            gather(1, s_gi, 1)

            def scatter(e):
                pool.wait_ge(s_gi, e + 1)
                pool.wait_ge(s_ys, e * 2 + 4)
                nc.gpsimd.tensor_copy(idx_s, idx[:, :, bass.ds(e, 1)].rearrange("p g o -> p (g o)")).then_inc(s_si, 1)
                pool.wait_ge(s_idx, 1)
                pool.wait_ge(s_si, e + 1)
                pool.indirect_dma_start(acc_d, bass.IndirectOffsetOnAxis(ap=idx_s[:, 0:1], axis=0), ys, None,
                                        compute_op=ALU.add).then_inc(s_scat, 16)
                pool.indirect_dma_start(acc_d, bass.IndirectOffsetOnAxis(ap=idx_s[0:CAP_P, 1:2], axis=0), ys_p[0:CAP_P, :], None,
                                        compute_op=ALU.add).then_inc(s_scat, 16)

            with pool.Fori(0, EXPERTS - 1) as e:
                scatter(e)
                pool.wait_ge(s_scat, e * 32 + 32)
                pool.wait_ge(s_xsT, e + 2)
                gather(e + 2, s_gi, e + 2)
            scatter(EXPERTS - 1)
            rstds(2 * TILES, 3 * TILES)


NAMES = ["x_prompt", "x_sample", "rel_bias_table", "w_in", "b_in", "gmlp_ln_g", "gmlp_ln_b", "gmlp_w_s", "gmlp_b_s",
         "w_out", "ln1_g", "ln1_b", "w_router", "w_gate", "w_up", "w_down", "ln2_g", "ln2_b"]


def kernel(**inputs):
    import concourse.bacc as bacc
    from concourse.bass_utils import run_bass_kernel_spmd

    nc = bacc.Bacc("TRN2", target_bir_lowering=False, num_devices=1)
    arrays, aps = {}, {}
    for name in NAMES + ["rel_rows"]:
        x = relative_rows() if name == "rel_rows" else np.ascontiguousarray(inputs[name])
        arrays["in_" + name] = x
        aps[name] = nc.dram_tensor("in_" + name, x.shape, mybir.dt.from_np(x.dtype), kind="ExternalInput").ap()
    outs = [nc.dram_tensor(n, (1, length, D), F32, kind="ExternalOutput").ap()
            for n, length in (("y_prompt", L_PROMPT), ("y_sample", L_SAMPLE))]
    build(nc, aps, outs)
    r = run_bass_kernel_spmd(nc, [arrays], core_ids=[0]).results[0]
    return r["y_prompt"], r["y_sample"]
```

```python
import math
from contextlib import ExitStack

import numpy as np
import concourse.bass as bass
from concourse import mybir

F32 = mybir.dt.float32
F32R = mybir.dt.float32r
U32 = mybir.dt.uint32
ALU = mybir.AluOpType
ACT = mybir.ActivationFunctionType
AX_X = mybir.AxisListType.X

P = 128
D = 1024
KT = D // P
L_PROMPT, L_SAMPLE = 256, 1024
TOKENS = L_PROMPT + L_SAMPLE
TILES = TOKENS // P
PT = L_PROMPT // P
HEADS, HD = 8, 64
AW = HEADS * HD
E_IN = 5 * AW
EXPERTS, FF = 16, 2816
FT = FF // P
CAP_P, CAP_S = 2 * L_PROMPT // EXPERTS, 2 * L_SAMPLE // EXPERTS
SLOTS = CAP_S + CAP_P
ALPHA = 2.0 ** 0.25
EPS = 1e-5
N_BUCKETS, MAX_DIST = 32, 1024
REL = 2 * L_SAMPLE
BIAS_W = L_SAMPLE - P + L_SAMPLE
MASKED = -1e30

PAIRS = FT // 2
GU_UNITS = 4 * PAIRS
DN_UNITS = PAIRS
UNITS = GU_UNITS + 2 * DN_UNITS
RING = 11
SPLIT = 6
W_COLS = 256
UW = 1024


def relative_rows():
    rel = (L_SAMPLE - 1) - np.arange(REL)
    half = N_BUCKETS // 2
    n = np.abs(rel)
    max_exact = half // 2
    large = max_exact + (np.log(np.maximum(n, 1) / max_exact) / np.log(MAX_DIST / max_exact)
                         * (half - max_exact)).astype(np.int32)
    bucket = np.where(rel > 0, half, 0) + np.where(n < max_exact, n, np.minimum(large, half - 1))
    count = sum(((n <= w // 2) & (n % d == 0)).astype(np.int64) for w, d in ((128, 1), (512, 4), (2048, 16)))
    rows = np.zeros((N_BUCKETS + 1, REL), np.float32)
    rows[bucket, np.arange(REL)] = 1.0
    rows[N_BUCKETS] = np.where(count > 0, np.log(np.maximum(count, 1)), MASKED)
    return rows


def build(nc, a, outs):
    out_prompt, out_sample = outs
    w_in, w_out = a["w_in"][0], a["w_out"][0]
    w_gate, w_up, w_down = a["w_gate"][0], a["w_up"][0], a["w_down"][0]
    x1_d = nc.dram_tensor("x1_rows", (TOKENS, D), F32, kind="Internal").ap()
    acc_d = nc.dram_tensor("acc_rows", (TOKENS, D), F32, kind="Internal").ap()
    rel_d = nc.dram_tensor("rel_bias", (HEADS, REL), F32, kind="Internal").ap()

    def token_rows(prompt, sample, t):
        return prompt[0, t * P:(t + 1) * P, :] if t < PT else sample[0, (t - PT) * P:(t - PT + 1) * P, :]

    with ExitStack() as ctx:
        def sem(name):
            return ctx.enter_context(nc.semaphore(name))

        psum = ctx.enter_context(nc.psum_tensor("banks", [P, 8, 512], F32))
        HI, LO = 0, 1

        def place(name, start, *shape, dt=F32):
            with ExitStack() as alone:
                if start:
                    alone.enter_context(nc.sbuf_tensor(name + "_below", [P, start], F32))
                return alone.enter_context(nc.sbuf_tensor(name, [P, *shape], dt))[(slice(None),) * (1 + len(shape))]

        x_parts = place("x_parts", 0, 2, KT, TOKENS, dt=F32R)
        win_parts = place("win_parts", 20480, 2, 2, KT, W_COLS, dt=F32R)
        win_raw = place("win_raw", 28672, 2, KT, W_COLS)
        qT_last = place("qT_last", 28672, 1, TOKENS)
        x_rows = place("x_rows", 32768, TILES, D)
        gm = place("gm", 32768, TILES, AW)
        v_rows = place("v_rows", 37888, TILES, AW)
        wsT = place("wsT", 37888, 2, 4, P)
        pre_t = place("pre_gelu", 38912, 2, 2 * W_COLS)
        pre = [pre_t[:, 0, :], pre_t[:, 1, :]]
        qT_first = place("qT_first", 43008, 3, TOKENS)
        rowb = place("uv_bias", 43008, 2, AW)
        gln = place("gmlp_ln", 44032, 2, AW)
        ws_rows = place("ws_rows", 45056, 8, P)
        kT = place("kT", 46848, 4, TOKENS)
        vn = place("vn", 46848, TILES, AW)
        rel_rows = place("rel_rows", 46848, REL)
        rel_bias = place("rel_table", 48896, REL)
        gln_g, gln_b = gln[:, 0, :], gln[:, 1, :]

        def q_tile(et):
            return qT_first[:, et, :] if et < 3 else qT_last[:, 0, :]

        relT = place("relT", 0, 2, BIAS_W)
        scored = place("scored", 3840, 2, L_SAMPLE)
        probs = place("probs", 5888, 3, L_SAMPLE)
        probsT = place("probsT", 8960, 2, KT, P)
        wout = place("wout_raw", 11008, KT, D)
        att = place("att", 20480, TILES, AW)
        ln1 = place("ln1", 25600, 2, D)
        ln1_g, ln1_b = ln1[:, 0, :], ln1[:, 1, :]
        wr = place("w_router", 27648, KT, EXPERTS)
        x_again = place("x_again", 29952, 2, D)
        wout_hi = place("wout_hi", 0, KT, D, dt=F32R)
        wout_lo = place("wout_lo", 37888, KT, D, dt=F32R)
        catT = place("catT_parts", 46080, 2, 2, KT, P, dt=F32R)
        ax1 = place("ax1", 8192, 2, D)
        resid = place("resid", 11008, 2, D)
        x1 = place("x1", 13056, 2, D)
        x1T = place("x1T", 15104, 2, KT, P)
        aff_ab = place("aff_rows", 17152, 2, L_SAMPLE)
        aff_a, aff_b = aff_ab[:, 0, :], aff_ab[:, 1, :]
        top = place("top", 19200, 3, CAP_S)
        top_val, top_idx, top_idf = top[:, 0, :], top[:, 1, :].bitcast(U32), top[:, 2, :]
        aff = place("aff", 19584, 2, EXPERTS)
        aff_e = place("aff_exp", 19616, 2, EXPERTS)
        gates = place("gates", 19648, 2, EXPERTS + 1)
        idx = place("idx", 19696, 2, EXPERTS + 1)[:, :, :].bitcast(U32)
        idx_g = place("idx_gather", 19744, 2)[:, :].bitcast(U32)
        idx_s = place("idx_scatter", 19760, 2)[:, :].bitcast(U32)
        sm = place("softmax_small", 19776, 4)
        smx, ssum = sm[:, 0:2], sm[:, 2:4]
        raw = place("raw_units", 0, RING, UW)
        ln2 = place("ln2", 11264, 2, D)
        ln2_g, ln2_b = ln2[:, 0, :], ln2[:, 1, :]
        w_parts = place("w_parts", 20480, 2, SPLIT, UW, dt=F32R)
        xs_parts = place("xs_parts", 32768, 2, KT, SLOTS, dt=F32R)
        h_parts = place("h_parts", 35328, 2, FT, SLOTS, dt=F32R)
        xs = place("xs", 42368, D)
        xs_p = place("xs_prompt", 43392, D)
        hid = place("hidden", 44416, 2, 2, SLOTS)
        sg = place("silu_gate", 45056, 2, 2, SLOTS)
        gate_sum = place("gate_sum", 45696, 2, 2, SLOTS)
        up_sum = place("up_sum", 46336, 2, SLOTS)
        yT = place("yT", 46656, KT, SLOTS)
        ys = place("ys", 47936, D)
        ys_p = place("ys_prompt", 48960, D)
        fin_in = place("fin_in", 20480, 5, D)
        fin_out = place("fin_out", 25600, 5, D)
        v_bias = place("v_bias", 51968, AW)
        ident = place("ident", 52480, P)
        table = place("table", 52608, HEADS)
        b_qk = place("b_qk", 52624, 8)
        b_s = place("b_s", 52640, 8)
        half_neg = place("half_neg", 52656, 1)
        veps = place("veps", 52672, 1)
        rstd = place("rstd", 52688, TILES)
        mv = place("mv", 52704, TILES, 2)
        stats = place("stats", 52736, 2, 6)
        mx = place("mx", 52752, 4)
        nmx = place("nmx", 52768, 4)
        den = place("den", 52784, 8)
        rden = place("rden", 52800, 2)
        lmx = place("lmx", 52816, 1)

        s_const, s_rel_in, s_bs, s_rows = sem("const_in"), sem("rel_in"), sem("small_in"), sem("rows_in")
        s_x = [sem(f"x_in{t}") for t in range(TILES)]
        s_win = [sem(f"win_in{i}") for i in range(2)]
        s_wh, s_wl, s_xh = sem("win_high"), sem("win_low"), sem("x_high")
        s_oh, s_ol, s_ch = sem("wout_high"), sem("wout_low"), sem("catT_high")
        s_ident, s_table1 = sem("ident_ready"), sem("table_one")
        s_job = sem("job_done")
        s_free = {"act": sem("freed_by_act"), "dve": sem("freed_by_dve")}
        s_rel_out, s_relT = sem("rel_stored"), [sem(f"relT_in{i}") for i in range(2)]
        s_gelu = sem("gelu_done")
        s_stat, s_rstd, s_vn = sem("stats_done"), sem("rstd_ready"), sem("vn_ready")
        s_pool = sem("pool_chain")
        s_dch = sem("dve_chain")
        s_bq = sem("bq_scaled")
        s_qk, s_scored, s_probs = sem("qk_done"), sem("scored"), sem("probs_ready")
        s_pt, s_ptc, s_pv, s_att = sem("probsT_done"), sem("probsT_copied"), sem("pv_done"), sem("att_out")
        s_wout, s_ln1, s_xa = sem("wout_in"), sem("ln1_in"), [sem(f"x_again{i}") for i in range(2)]
        s_catT, s_catTc, s_mix = sem("catT_done"), sem("catT_copied"), sem("mix_done")
        s_res = sem("resid_done")
        s_x1, s_ax1, s_x1st = sem("x1_ready"), sem("ax1_ready"), [sem(f"x1_stored{i}") for i in range(2)]
        s_x1T, s_x1Tc, s_log = sem("x1T_done"), sem("x1T_copied"), sem("logits_done")
        s_smx, s_sexp, s_aff, s_affT, s_affTc = (sem("logit_max"), sem("logit_exp"), sem("aff_ready"),
                                                 sem("affT_done"), sem("affT_copied"))
        s_top, s_topT, s_idx = sem("top_ready"), sem("topT_done"), sem("idx_ready")
        s_unit_in = [sem(f"unit_in{i}") for i in range(RING)]
        s_unit = sem("units_done")
        s_hi, s_lo = sem("unit_high"), sem("unit_low")
        s_gate, s_up = sem("gate_summed"), sem("up_summed")
        s_silu, s_mul, s_hh, s_hid = sem("silu_done"), sem("hidden_done"), sem("hidden_high"), sem("hidden_low")
        s_gath = sem("gathered")
        s_xsT, s_xsH, s_xsL = sem("xsT_done"), sem("xs_high"), sem("xs_low")
        s_yT, s_yt, s_ys = sem("yT_copied"), sem("y_transposed"), sem("ys_ready")
        s_scat, s_gi0, s_gi, s_si = sem("scattered"), sem("first_idx"), sem("gather_idx"), sem("scatter_idx")
        s_fin_in = [sem(f"fin_in{i}") for i in range(5)]
        s_ln2, s_fin, s_out = sem("ln2_in"), sem("fin_ready"), [sem(f"out_stored{i}") for i in range(5)]

        jobs = [("rel", i, "dve") for i in range(4)]
        jobs += [("xT", (t, i), "dve") for t in range(TILES) for i in range(2)]
        jobs += [("ws", i, "act") for i in range(2)]
        CH = [(0, 512), (512, 512), (1024, 256)]
        BLOCKS = [("gv", 4 * AW), ("gu", 3 * AW), ("v", 2 * AW), ("k", AW), ("q", 0)]
        WUNITS = [(name, half, c + half * W_COLS) for name, c in BLOCKS for half in range(AW // W_COLS)]
        for name, half, _ in WUNITS:
            if (name, half) == ("v", 0):
                jobs += [("gm", t, "dve") for t in range(TILES)]
            if name in ("q", "k"):
                jobs += [(name, (2 * half + j, c), "act") for j in range(2) for c in range(3)]
            else:
                jobs += [(name, (half, t), "dve") for t in range(TILES)]
        freed = []
        for n, (_, _, eng) in enumerate(jobs):
            freed.append(1 + sum(e == eng for _, _, e in jobs[:n]))

        unit_jobs = [1 + max(n for n, j in enumerate(jobs) if j[0] == name and
                             (j[1][0] // 2 == half if name in ("q", "k") else j[1][0] == half))
                     for name, half, _ in WUNITS]

        units = [(h, g, qt) for h in range(HEADS) for g in range(2)
                 for qt in range(PT if g == 0 else TILES - PT)]
        NU = len(units)
        glen = (L_PROMPT, L_SAMPLE)
        gtile = (0, PT)

        block = ctx.enter_context(nc.Block())

        def unit_src(e, u):
            if u < GU_UNITS:
                pr, kind = u // 4, u % 4
                w = (w_gate, w_up)[kind // 2]
                k0 = (kind % 2) * (KT // 2) * P
                return w[e, k0:k0 + KT // 2 * P, pr * 2 * P:(pr + 1) * 2 * P].rearrange("(k p) f -> p k f", p=P)
            half, pr = divmod(u - GU_UNITS, DN_UNITS)
            return w_down[e, pr * 2 * P:(pr + 1) * 2 * P, half * 512:(half + 1) * 512].rearrange("(k p) f -> p k f", p=P)

        def unit_dst(u):
            k = KT // 2 if u % UNITS < GU_UNITS else 2
            return raw[:, u % RING, :].rearrange("p (k f) -> p k f", k=k)

        @block.sync
        def _(sp):
            def load_win(n):
                if n >= 2:
                    sp.wait_ge(s_wl, n - 1)
                c = WUNITS[n][2]
                sp.dma_start(win_raw[:, n % 2], w_in[:, c:c + W_COLS].rearrange("(k p) f -> p k f", p=P)).then_inc(s_win[n % 2], 16)

            for t in range(TILES):
                sp.dma_start(x_rows[:, t], token_rows(a["x_prompt"], a["x_sample"], t)).then_inc(s_x[t], 16)
                if t in (3, 7):
                    load_win(t // 4)
            sp.wait_ge(s_free["dve"], 4)
            sp.dma_start(rel_d[:, :], rel_bias[0:HEADS, :]).then_inc(s_rel_out, 16)
            for n in range(2, len(WUNITS)):
                load_win(n)
            sp.wait_ge(s_job, len(jobs))
            sp.wait_ge(s_rel_out, 16)

            def load_relT(h):
                if h >= 2:
                    sp.wait_ge(s_scored, 10 * (h - 1))
                src = bass.AP(tensor=rel_d.tensor, offset=h * REL, ap=[[1, P], [1, BIAS_W]])
                sp.dma_start(relT[:, h % 2, :], src).then_inc(s_relT[h % 2], 16)

            load_relT(0)
            load_relT(1)
            sp.dma_start(wout[:, :, :], w_out.rearrange("(k p) f -> p k f", p=P)).then_inc(s_wout, 16)
            for i, name in enumerate(("ln1_g", "ln1_b")):
                sp.dma_start(ln1[:, i, :], a[name][0:1, :].to_broadcast([P, D])).then_inc(s_ln1, 16)
            sp.dma_start(wr, a["w_router"][0].rearrange("(k p) e -> p k e", p=P)).then_inc(s_ln1, 16)

            def load_x(t):
                if t >= 2:
                    sp.wait_ge(s_res, t - 1)
                sp.dma_start(x_again[:, t % 2], token_rows(a["x_prompt"], a["x_sample"], t)).then_inc(s_xa[t % 2], 16)

            load_x(0)
            load_x(1)
            for h in range(2, HEADS):
                load_relT(h)
            for t in range(TILES):
                if t + 2 < TILES:
                    load_x(t + 2)
                sp.wait_ge(s_x1, t + 1)
                sp.dma_start(x1_d[t * P:(t + 1) * P, :], x1[:, t % 2]).then_inc(s_x1st[t % 2], 16)
                sp.wait_ge(s_ax1, t + 1)
                sp.dma_start(acc_d[t * P:(t + 1) * P, :], ax1[:, t % 2]).then_inc(s_x1st[t % 2], 16)
            for i in range(2):
                sp.wait_ge(s_x1st[i], 32 * (TILES // 2))
            for u in range(RING):
                sp.dma_start(unit_dst(u), unit_src(0, u)).then_inc(s_unit_in[u], 16)
            for i, name in enumerate(("ln2_g", "ln2_b")):
                sp.dma_start(ln2[:, i, :], a[name][0:1, :].to_broadcast([P, D])).then_inc(s_ln2, 16)

            with sp.Fori(0, EXPERTS - 1) as e:
                for u in range(UNITS):
                    n = u + RING
                    if n % UNITS not in (0, 2, GU_UNITS):
                        sp.wait_ge(s_lo, e * UNITS + (u + 1 + ((n + 1) % UNITS in (0, 2, GU_UNITS))))
                    sp.dma_start(unit_dst(n), unit_src(e + n // UNITS, n % UNITS)).then_inc(s_unit_in[n % RING], 16)
            for u in range(UNITS - RING):
                n = u + RING
                sp.wait_ge(s_lo, (EXPERTS - 1) * UNITS + u + 1)
                sp.dma_start(unit_dst(n), unit_src(EXPERTS - 1, n)).then_inc(s_unit_in[n % RING], 16)

            sp.wait_ge(s_scat, 32 * EXPERTS)
            for t in range(TILES + 3):
                if t < TILES:
                    if t >= 5:
                        sp.wait_ge(s_fin, t - 4)
                    sp.dma_start(fin_in[:, t % 5], acc_d[t * P:(t + 1) * P, :]).then_inc(s_fin_in[t % 5], 16)
                if t >= 3:
                    sp.wait_ge(s_fin, t - 2)
                    sp.dma_start(token_rows(out_prompt, out_sample, t - 3), fin_out[:, (t - 3) % 5]).then_inc(s_out[(t - 3) % 5], 16)
            for i in range(5):
                sp.wait_ge(s_out[i], 16 * (TILES // 5))

        @block.tensor
        def _(pe):
            pe.wait_ge(s_ident, 2)
            jn = [0]
            waited = {"act": 0, "dve": 0}

            def job(name):
                n = jn[0]
                assert jobs[n][0] == name
                if n >= 8:
                    eng, c = jobs[n - 8][2], freed[n - 8]
                    if c > waited[eng]:
                        pe.wait_ge(s_free[eng], c)
                        waited[eng] = c
                jn[0] += 1
                return psum[:, n % 8, :], jobs[n][1]

            pe.wait_ge(s_rel_in, 32)
            pe.wait_ge(s_table1, 1)
            for i in range(4):
                bank, _ = job("rel")
                nc.tensor.matmul(bank[0:HEADS, :], table[0:N_BUCKETS + 1, :], rel_rows[0:N_BUCKETS + 1, i * 512:(i + 1) * 512],
                                 start=True, stop=True).then_inc(s_job, 1)
            for t in range(TILES):
                pe.wait_ge(s_x[t], 16)
                for i in range(2):
                    bank, _ = job("xT")
                    for k in range(4):
                        last = nc.tensor.transpose(bank[:, k * P:(k + 1) * P], x_rows[:, t, (4 * i + k) * P:(4 * i + k + 1) * P], ident)
                    last.then_inc(s_job, 1)
            pe.wait_ge(s_rows, 16)
            for i in range(2):
                bank, _ = job("ws")
                for g in range(4):
                    last = nc.tensor.transpose(bank[:, g * P:(g + 1) * P], ws_rows[:, 4 * i + g, :], ident)
                last.then_inc(s_job, 1)
            pe.wait_ge(s_free["dve"], freed[3 + 2 * TILES])

            def three_parts(out, w_of, x_of, first, last_one):
                for n, (wp, xp) in enumerate(((HI, HI), (HI, LO), (LO, HI))):
                    last = nc.tensor.matmul(out, w_of(wp), x_of(xp), start=first and n == 0, stop=last_one and n == 2)
                return last

            for u, (name, half, _) in enumerate(WUNITS):
                if (name, half) == ("v", 0):
                    for t in range(TILES):
                        bank, _ = job("gm")
                        pe.wait_ge(s_vn, t + 1)
                        for g in range(8):
                            last = nc.tensor.matmul(bank[:, g * HD:(g + 1) * HD], wsT[:, g // 4, g % 4, :],
                                                    vn[:, t, g * HD:(g + 1) * HD], start=True, stop=True)
                        last.then_inc(s_job, 1)
                pe.wait_ge(s_wl, u + 1)
                w = win_parts[:, :, u % 2]
                if name in ("q", "k"):
                    for j in range(2):
                        for c0, cn in CH:
                            bank, _ = job(name)
                            for k in range(KT):
                                last = three_parts(bank[:, 0:cn], lambda p: w[:, p, k, j * P:(j + 1) * P],
                                                   lambda p: x_parts[:, p, k, c0:c0 + cn], k == 0, k == KT - 1)
                            last.then_inc(s_job, 1)
                else:
                    for t in range(TILES):
                        bank, _ = job(name)
                        for k in range(KT):
                            last = three_parts(bank[:, 0:W_COLS], lambda p: x_parts[:, p, k, t * P:(t + 1) * P],
                                               lambda p: w[:, p, k, :], k == 0, k == KT - 1)
                        last.then_inc(s_job, 1)

            for eng in ("act", "dve"):
                pe.wait_ge(s_free[eng], sum(e == eng for _, _, e in jobs))
            for n in range(NU + 3):
                if n < NU:
                    h, g, qt = units[n]
                    if n >= 2:
                        pe.wait_ge(s_scored, n - 1)
                    base, t0 = HD * (h % 2), gtile[g] * P
                    q = q_tile(h // 2)[base:base + HD, t0 + qt * P:t0 + (qt + 1) * P]
                    for c in range(0, glen[g], 512):
                        cn = min(512, glen[g])
                        last = nc.tensor.matmul(psum[:, 2 * (n % 2) + c // 512, 0:cn], q,
                                                kT[base:base + HD, h // 2, t0 + c:t0 + c + cn], start=True, stop=True)
                    last.then_inc(s_qk, 1)
                if 0 <= n - 2 < NU:
                    m = n - 2
                    pe.wait_ge(s_probs, m + 1)
                    if m >= 1:
                        pe.wait_ge(s_ptc, m)
                    for kt in range(glen[units[m][1]] // P):
                        last = nc.tensor.transpose(psum[:, 4 + kt // 4, kt % 4 * P:(kt % 4 + 1) * P],
                                                   probs[:, m % 3, kt * P:(kt + 1) * P], ident)
                    last.then_inc(s_pt, 1)
                if 0 <= n - 3 < NU:
                    m = n - 3
                    h, g, qt = units[m]
                    pe.wait_ge(s_ptc, m + 1)
                    if m >= 2:
                        pe.wait_ge(s_att, m - 1)
                    nk = glen[g] // P
                    for kt in range(nk):
                        last = nc.tensor.matmul(psum[:, 6 + m % 2, 0:HD], probsT[:, m % 2, kt, :],
                                                v_rows[:, gtile[g] + kt, h * HD:(h + 1) * HD],
                                                start=kt == 0, stop=kt == nk - 1)
                    last.then_inc(s_pv, 1)

            pe.wait_ge(s_att, NU)
            pe.wait_ge(s_ln1, 48)

            def cat_transposes(t):
                if t >= 1:
                    pe.wait_ge(s_catTc, t)
                for k in range(KT):
                    src = (att if k < KT // 2 else gm)[:, t, k % (KT // 2) * P:(k % (KT // 2) + 1) * P]
                    last = nc.tensor.transpose(psum[:, k // 4, k % 4 * P:(k % 4 + 1) * P], src, ident)
                last.then_inc(s_catT, 1)

            def mix(t, j):
                if j == 0:
                    pe.wait_ge(s_catTc, t + 1)
                    if t >= 2:
                        pe.wait_ge(s_res, t - 1)
                for k in range(KT):
                    if t == 0 and j == 0:
                        pe.wait_ge(s_ol, k + 1)
                    last = three_parts(psum[:, 2 + 2 * (t % 2) + j, :], lambda p: catT[:, p, t % 2, k, :],
                                       lambda p: (wout_hi, wout_lo)[p][:, k, j * 512:(j + 1) * 512], k == 0, k == KT - 1)
                if j == 1:
                    last.then_inc(s_mix, 1)

            def x1_transposes(t):
                pe.wait_ge(s_x1, t + 1)
                if t >= 1:
                    pe.wait_ge(s_smx, t)
                    pe.wait_ge(s_sexp, t)
                    pe.wait_ge(s_affTc, t)
                for k in range(KT):
                    last = nc.tensor.transpose(psum[:, 6 + k // 4, k % 4 * P:(k % 4 + 1) * P], x1[:, t % 2, k * P:(k + 1) * P], ident)
                last.then_inc(s_x1T, 1)

            def logits(t):
                pe.wait_ge(s_x1Tc, t + 1)
                for k in range(KT):
                    last = nc.tensor.matmul(psum[:, 6, 0:EXPERTS], x1T[:, t % 2, k, :], wr[:, k, :], start=k == 0, stop=k == KT - 1)
                last.then_inc(s_log, 1)

            def aff_transpose(t):
                pe.wait_ge(s_aff, t + 1)
                if t >= 1:
                    pe.wait_ge(s_affTc, t)
                nc.tensor.transpose(psum[0:EXPERTS, 7, 0:P], aff[:, t % 2, :], ident).then_inc(s_affT, 1)

            cat_transposes(0)
            for t in range(TILES + 1):
                if t < TILES:
                    mix(t, 0)
                if t >= 2:
                    aff_transpose(t - 2)
                if t >= 1:
                    x1_transposes(t - 1)
                if t + 1 < TILES:
                    cat_transposes(t + 1)
                if t < TILES:
                    mix(t, 1)
                if t >= 1:
                    logits(t - 1)
            aff_transpose(TILES - 1)

            pe.wait_ge(s_top, 1)
            nc.tensor.transpose(psum[:, 0, 0:48], top_val[0:48, :], ident[0:48, 0:48])
            nc.tensor.transpose(psum[:, 1, 0:48], top_idf[0:48, :], ident[0:48, 0:48]).then_inc(s_topT, 1)

            def xs_transposes():
                for k in range(KT):
                    o0 = k % 3 * SLOTS
                    nc.tensor.transpose(psum[:, k // 3, o0:o0 + CAP_S], xs[:, k * P:(k + 1) * P], ident)
                    last = nc.tensor.transpose(psum[:, k // 3, o0 + CAP_S:o0 + SLOTS], xs_p[0:CAP_P, k * P:(k + 1) * P],
                                               ident[0:CAP_P, 0:CAP_P])
                last.then_inc(s_xsT, 1)

            def y_transposes(half, bank_s, bank_p):
                for i in range(4):
                    nc.tensor.transpose(psum[:, bank_s, i * P:(i + 1) * P], yT[:, 4 * half + i, 0:CAP_S], ident)
                    last = nc.tensor.transpose(psum[0:CAP_P, bank_p, i * P:(i + 1) * P], yT[:, 4 * half + i, CAP_S:SLOTS], ident)
                last.then_inc(s_yt, 1)

            pe.wait_ge(s_idx, 1)
            pe.wait_ge(s_gath, 32)
            xs_transposes()
            def product(bank, u, cols, moving, first, last_one):
                nc.tensor.matmul(bank[:, 0:2 * SLOTS], w_parts[:, HI, u % SPLIT, cols], moving(slice(HI, LO + 1)),
                                 start=first, stop=False)
                return nc.tensor.matmul(bank[:, 0:SLOTS], w_parts[:, LO, u % SPLIT, cols], moving(HI), start=False, stop=last_one)

            pe.sem_inc(s_unit, SPLIT)
            with pe.Fori(0, EXPERTS) as e:
                pe.wait_ge(s_xsL, e + 1)
                pe.wait_ge(s_ys, e * 2 + 1)
                for pr in range(PAIRS):
                    for kind in range(4):
                        u = 4 * pr + kind
                        pe.wait_ge(s_lo, e * UNITS + (u + 1))
                        if kind == 0:
                            pe.wait_ge(s_gate, e * PAIRS + (pr + 1))
                        if kind == 2:
                            pe.wait_ge(s_mul, e * PAIRS + (pr + 1))
                        for j in range(2):
                            for k in range(KT // 2):
                                kk = kind % 2 * (KT // 2) + k
                                last = product(psum[:, 2 * (kind // 2) + j, :], u, slice((2 * k + j) * P, (2 * k + j + 1) * P),
                                               lambda part, kk=kk: xs_parts[:, part, kk, :], kk == 0, kk == KT - 1)
                        last.then_inc(s_unit, 1)
                    if pr == 1:
                        pe.wait_ge(s_yT, e * 8 + 4)
                        y_transposes(1, 4, 5)
                for half in range(2):
                    for pr in range(PAIRS):
                        u = GU_UNITS + DN_UNITS * half + pr
                        pe.wait_ge(s_lo, e * UNITS + (u + 1))
                        if half == 0:
                            pe.wait_ge(s_hid, e * PAIRS + (pr + 2))
                            if pr == 0:
                                pe.wait_ge(s_ys, e * 2 + 2)
                        order = [(j, i) for j in range(2) for i in range(4)] if pr < PAIRS - 1 else \
                                [(j, i) for i in range(4) for j in range(2)]
                        for j, i in order:
                            if pr == 0 and half == 1 and j == 0:
                                pe.wait_ge(s_yT, e * 8 + (5 + i))
                            last = product(psum[:, 4 + i, :], u, slice((4 * j + i) * P, (4 * j + i + 1) * P),
                                           lambda part, f=2 * pr + j: h_parts[:, part, f, :],
                                           pr == 0 and j == 0, pr == PAIRS - 1 and j == 1)
                        last.then_inc(s_unit, 1)
                        if half == 0 and pr == 1:
                            pe.wait_ge(s_mul, e * PAIRS + (PAIRS + 1))
                            pe.wait_ge(s_gath, e * 32 + 64)
                            xs_transposes()
                        if half == 1 and pr == 2:
                            pe.wait_ge(s_xsL, e + 2)
                            pe.wait_ge(s_yT, e * 8 + 8)
                            y_transposes(0, 3, 0)
            pe.wait_ge(s_yT, EXPERTS * 8 + 4)
            pe.wait_ge(s_ys, EXPERTS * 2 + 1)
            y_transposes(1, 4, 5)

        @block.scalar
        def _(act):
            act.dma_start(rel_rows[0:N_BUCKETS + 1, :], a["rel_rows"]).then_inc(s_rel_in, 16)
            act.dma_start(table[0:N_BUCKETS, :], a["rel_bias_table"]).then_inc(s_rel_in, 16)
            act.dma_start(ws_rows, a["gmlp_w_s"][0].rearrange("g p q -> p g q")).then_inc(s_rows, 16)
            act.dma_start(v_bias, a["b_in"][0:1, 2 * AW:3 * AW].to_broadcast([P, AW])).then_inc(s_const, 16)
            act.dma_start(rowb, a["b_in"][0:1, 3 * AW:5 * AW].to_broadcast([P, 2 * AW])
                          .rearrange("p (a b) -> p a b", a=2)).then_inc(s_const, 16)
            act.dma_start(gln_g, a["gmlp_ln_g"][0:1, :].to_broadcast([P, AW])).then_inc(s_const, 16)
            act.dma_start(gln_b, a["gmlp_ln_b"][0:1, :].to_broadcast([P, AW])).then_inc(s_const, 16)
            act.dma_start(b_qk, a["b_in"][0, 0:2 * AW].rearrange("(e p) -> p e", p=P),
                          allow_slow_non_contiguous=True).then_inc(s_bs, 16)
            act.dma_start(b_s, a["gmlp_b_s"][0].rearrange("g p -> p g"),
                          allow_slow_non_contiguous=True).then_inc(s_bs, 16)
            act.wait_ge(s_bs, 32)
            nc.scalar.mul(b_qk[:, 0:4], b_qk[:, 0:4], HD ** -0.5).then_inc(s_bq, 1)

            def split_win(u):
                act.wait_ge(s_win[u % 2], 16 * (u // 2 + 1))
                if u >= 2:
                    act.wait_ge(s_job, unit_jobs[u - 2])
                nc.scalar.copy(win_parts[:, HI, u % 2], win_raw[:, u % 2]).then_inc(s_wh, 1)

            gel, unit = 0, 0
            for n, (name, arg, eng) in enumerate(jobs):
                if name == "xT":
                    t, i = arg
                    act.wait_ge(s_job, n + 1)
                    nc.scalar.copy(x_parts[:, HI, 4 * i:4 * i + 4, t * P:(t + 1) * P],
                                   psum[:, n % 8, :].rearrange("p (k c) -> p k c", k=4)).then_inc(s_xh, 1)
                    if arg == (TILES - 1, 1):
                        split_win(0)
                        split_win(1)
                        unit = 2
                    continue
                if unit >= 2 and unit < len(WUNITS) and n == unit_jobs[unit - 2] + 1:
                    split_win(unit)
                    unit += 1
                if name in ("gv", "gu"):
                    half, t = arg
                    act.wait_ge(s_free["dve"], freed[n])
                    dst = (vn if name == "gv" else gm)[:, t, half * W_COLS:(half + 1) * W_COLS]
                    if gel == 0:
                        act.wait_ge(s_rel_out, 16)
                    nc.scalar.activation(dst, pre[gel % 2][:, 0:W_COLS], ACT.Gelu_apprx_tanh).then_inc(s_gelu, 1)
                    gel += 1
                if eng != "act":
                    continue
                act.wait_ge(s_job, n + 1)
                bank = psum[:, n % 8, :]
                if name == "ws":
                    nc.scalar.copy(wsT[:, arg], bank.rearrange("p (g q) -> p g q", q=P)).then_inc(s_free["act"], 1)
                else:
                    et, c = arg
                    c0, cn = CH[c]
                    if name == "q" and arg == (0, 0):
                        act.wait_ge(s_bq, 1)
                    dst = (q_tile(et) if name == "q" else kT[:, et, :])[:, c0:c0 + cn]
                    b = b_qk[:, et:et + 1] if name == "q" else b_qk[:, 4 + et:5 + et]
                    nc.scalar.activation(dst, bank[:, 0:cn], ACT.Identity, bias=b,
                                         scale=HD ** -0.5 if name == "q" else 1.0).then_inc(s_free["act"], 1)

            for n in range(NU + 2):
                if n >= 2:
                    m = n - 2
                    act.wait_ge(s_pt, m + 1)
                    if m >= 2:
                        act.wait_ge(s_pv, m - 1)
                    nk = glen[units[m][1]] // P
                    src = psum[:, 4:6, :].rearrange("p b (k c) -> p (b k) c", c=P)[:, 0:nk, :]
                    nc.scalar.copy(probsT[:, m % 2, 0:nk, :], src).then_inc(s_ptc, 1)
                if n < NU:
                    L = glen[units[n][1]]
                    act.wait_ge(s_scored, n + 1)
                    if n >= 3:
                        act.wait_ge(s_pt, n - 2)
                    nc.scalar.activation(probs[:, n % 3, 0:L], scored[:, n % 2, 0:L], ACT.Exp, bias=nmx[:, n % 4:n % 4 + 1],
                                         scale=1.0, accum_out=den[:, n % 8:n % 8 + 1]).then_inc(s_probs, 1)

            def cat_copy(t):
                act.wait_ge(s_catT, t + 1)
                if t >= 2:
                    act.wait_ge(s_mix, t - 1)
                nc.scalar.copy(catT[:, HI, t % 2], psum[:, 0:2, :].rearrange("p b (k c) -> p (b k) c", c=P)).then_inc(s_ch, 1)

            act.wait_ge(s_pv, NU)
            act.wait_ge(s_wout, 16)
            cat_copy(0)
            for k in range(KT):
                nc.scalar.copy(wout_hi[:, k, :], wout[:, k, :]).then_inc(s_oh, 1)
            for t in range(TILES + 1):
                if t >= 1:
                    m = t - 1
                    act.wait_ge(s_x1, m + 1)
                    if m >= 2:
                        act.wait_ge(s_x1st[m % 2], 32 * (m // 2))
                    nc.scalar.mul(ax1[:, m % 2], x1[:, m % 2], ALPHA).then_inc(s_ax1, 1)
                    act.wait_ge(s_x1T, m + 1)
                    if m >= 2:
                        act.wait_ge(s_log, m - 1)
                    nc.scalar.copy(x1T[:, m % 2], psum[:, 6:8, :].rearrange("p b (k c) -> p (b k) c", c=P)).then_inc(s_x1Tc, 1)
                if t + 1 < TILES:
                    cat_copy(t + 1)
                if t >= 1:
                    m = t - 1
                    act.wait_ge(s_smx, m + 1)
                    if m >= 2:
                        act.wait_ge(s_aff, m - 1)
                    nc.scalar.activation(aff_e[:, m % 2], psum[:, 6, 0:EXPERTS], ACT.Exp, bias=smx[:, m % 2:m % 2 + 1], scale=1.0,
                                         accum_out=ssum[:, m % 2:m % 2 + 1]).then_inc(s_sexp, 1)

            def xs_copy(e_done):
                act.wait_ge(s_xsT, e_done)
                for b in range(3):
                    nk = min(3, KT - 3 * b)
                    last = nc.scalar.copy(xs_parts[:, HI, 3 * b:3 * b + nk, :], psum[:, b, 0:nk * SLOTS].rearrange("p (k c) -> p k c", k=nk))
                last.then_inc(s_xsH, 1)

            def ys_copy(half, bank_s, bank_p, gate_s, gate_p):
                c = slice(512 * half, 512 * half + 512)
                nc.scalar.activation(ys[:, c], psum[:, bank_s, :], ACT.Copy, scale=gate_s)
                nc.scalar.activation(ys_p[0:CAP_P, c], psum[0:CAP_P, bank_p, :], ACT.Copy, scale=gate_p).then_inc(s_ys, 1)

            act.wait_ge(s_idx, 1)
            xs_copy(1)
            act.sem_inc(s_silu, 1)
            act.sem_inc(s_ys, 1)
            with act.Fori(0, EXPERTS) as e:
                for u in range(UNITS):
                    act.wait_ge(s_unit_in[u % RING], e * (16 * UNITS // RING) + 16 * (u // RING + 1))
                    act.wait_ge(s_unit, e * UNITS + (u + 1))
                    nc.scalar.copy(w_parts[:, HI, u % SPLIT, :], raw[:, u % RING, :]).then_inc(s_hi, 1)
                    if u % 4 == 3 and 7 <= u <= GU_UNITS + 3:
                        pr = (u - 7) // 4
                        act.wait_ge(s_gate, e * PAIRS + (pr + 2))
                        act.wait_ge(s_mul, e * PAIRS + max(pr, 1))
                        nc.scalar.activation(sg[:, pr % 2], gate_sum[:, pr % 2], ACT.Silu).then_inc(s_silu, 1)
                    if u % 4 == 1 and 9 <= u <= GU_UNITS + 5:
                        pr = (u - 9) // 4
                        act.wait_ge(s_mul, e * PAIRS + (pr + 2))
                        nc.scalar.copy(h_parts[:, HI, 2 * pr:2 * pr + 2, :], hid[:, pr % 2]).then_inc(s_hh, 1)
                    if u == 13:
                        act.wait_ge(s_yt, e * 2 + 1)
                        ys_copy(1, 4, 5, gates[:, 0, bass.ds(e, 1)], gates[0:CAP_P, 1, bass.ds(e, 1)])
                    if u == GU_UNITS + 7:
                        xs_copy(e + 2)
                    if u == GU_UNITS + DN_UNITS + 8:
                        act.wait_ge(s_yt, e * 2 + 2)
                        act.wait_ge(s_gi, e + 1)
                        ys_copy(0, 3, 0, gates[:, 0, bass.ds(e + 1, 1)], gates[0:CAP_P, 1, bass.ds(e + 1, 1)])
            act.wait_ge(s_yt, EXPERTS * 2 + 1)
            ys_copy(1, 4, 5, gates[:, 0, EXPERTS:EXPERTS + 1], gates[0:CAP_P, 1, EXPERTS:EXPERTS + 1])

        @block.vector
        def _(dve):
            chain = [0]

            def link(ins):
                chain[0] += 1
                ins.then_inc(s_dch, 1)
                dve.wait_ge(s_dch, chain[0])

            nc.vector.memset(table[N_BUCKETS:N_BUCKETS + 1, :], 1.0).then_inc(s_table1, 1)

            def gmlp_stats(t):
                dve.wait_ge(s_gelu, TILES + t + 1)
                if t:
                    dve.wait_ge(s_stat, t)
                link(nc.vector.bn_stats(stats[:, 0, :], vn[:, t, :]))
                nc.vector.bn_aggr(mv[:, t, :], stats[:, 0, :]).then_inc(s_stat, 1)

            def gmlp_norm(t):
                dve.wait_ge(s_rstd, t + 1)
                link(nc.vector.scalar_tensor_tensor(vn[:, t, :], vn[:, t, :], mv[:, t, 0:1], gln_g, ALU.subtract, ALU.mult))
                nc.vector.scalar_tensor_tensor(vn[:, t, :], vn[:, t, :], rstd[:, t:t + 1], gln_b, ALU.mult, ALU.add).then_inc(s_vn, 1)

            def low(out, whole, high):
                return nc.vector.tensor_tensor(out, whole, high.bitcast(F32), ALU.subtract)

            def split_win(u):
                dve.wait_ge(s_wh, u + 1)
                low(win_parts[:, LO, u % 2], win_raw[:, u % 2], win_parts[:, HI, u % 2]).then_inc(s_wl, 1)

            nat, unit = 0, 0
            for n, (name, arg, eng) in enumerate(jobs):
                if 2 <= unit < len(WUNITS) and n == unit_jobs[unit - 2] + 1:
                    split_win(unit)
                    unit += 1
                if eng != "dve":
                    continue
                dve.wait_ge(s_job, n + 1)
                bank = psum[:, n % 8, :]
                done = lambda ins: ins.then_inc(s_free["dve"], 1)
                if name == "rel":
                    done(nc.vector.tensor_copy(rel_bias[0:HEADS, arg * 512:(arg + 1) * 512], bank[0:HEADS, :]))
                elif name == "xT":
                    t, i = arg
                    dve.wait_ge(s_xh, n - 3)
                    ks, ts = slice(4 * i, 4 * i + 4), slice(t * P, (t + 1) * P)
                    done(low(x_parts[:, LO, ks, ts], bank.rearrange("p (k c) -> p k c", k=4), x_parts[:, HI, ks, ts]))
                    if arg == (TILES - 1, 1):
                        split_win(0)
                        split_win(1)
                        unit = 2
                elif name in ("gv", "gu"):
                    half, t = arg
                    cols = slice(half * W_COLS, (half + 1) * W_COLS)
                    if nat == 0:
                        dve.wait_ge(s_const, 64)
                    if nat >= 2:
                        dve.wait_ge(s_gelu, nat - 1)
                    done(nc.vector.tensor_tensor(pre[nat % 2][:, 0:W_COLS], bank[:, 0:W_COLS], rowb[:, 1 if name == "gv" else 0, cols], ALU.add))
                    if TILES + 1 <= nat <= 2 * TILES:
                        gmlp_stats(nat - TILES - 1)
                    if TILES + 2 <= nat <= 2 * TILES + 1:
                        gmlp_norm(nat - TILES - 2)
                    nat += 1
                elif name == "gm":
                    if arg == 0:
                        dve.wait_ge(s_bs, 32)
                        dve.wait_ge(s_gelu, 4 * TILES)
                    g = vn[:, arg, :]
                    link(nc.vector.tensor_tensor(g.rearrange("p (g c) -> p g c", c=HD), bank.rearrange("p (g c) -> p g c", c=HD),
                                                 b_s.unsqueeze(2).to_broadcast([P, 8, HD]), ALU.add))
                    done(nc.vector.tensor_tensor(gm[:, arg, :], gm[:, arg, :], g, ALU.mult))
                elif name == "v":
                    half, t = arg
                    cols = slice(half * W_COLS, (half + 1) * W_COLS)
                    done(nc.vector.tensor_tensor(v_rows[:, t, cols], bank[:, 0:W_COLS], v_bias[:, cols], ALU.add))

            for n in range(NU + 4):
                if n < NU:
                    h, g, qt = units[n]
                    L = glen[g]
                    dve.wait_ge(s_qk, n + 1)
                    if n >= 2:
                        dve.wait_ge(s_probs, n - 1)
                    if g == 0 and qt == 0:
                        dve.wait_ge(s_relT[h % 2], 16 * (h // 2 + 1))
                    hi = qt * P + L_SAMPLE - 1
                    lo = hi - (L - 1)
                    bias = relT[:, h % 2, lo:hi + 1][:, ::-1]
                    src = psum[:, 2 * (n % 2):2 * (n % 2) + 2, :].rearrange("p b c -> p (b c)")[:, 0:L]
                    link(nc.vector.tensor_tensor_reduce(out=scored[:, n % 2, 0:L], in0=src, in1=bias, scale=1.0, scalar=-3e38,
                                                        op0=ALU.add, op1=ALU.max, accum_out=mx[:, n % 4:n % 4 + 1]))
                    nc.vector.tensor_scalar(nmx[:, n % 4:n % 4 + 1], mx[:, n % 4:n % 4 + 1], -1.0, None, ALU.mult).then_inc(s_scored, 1)
                if n >= 4:
                    m = n - 4
                    h, g, qt = units[m]
                    dve.wait_ge(s_pv, m + 1)
                    if m >= 2:
                        dve.wait_ge(s_att, m - 1)
                    link(nc.vector.reciprocal(rden[:, m % 2:m % 2 + 1], den[:, m % 8:m % 8 + 1]))
                    nc.vector.tensor_scalar(att[:, gtile[g] + qt, h * HD:(h + 1) * HD], psum[:, 6 + m % 2, 0:HD],
                                            rden[:, m % 2:m % 2 + 1], None,
                                            ALU.mult).then_inc(s_att, 1)


            def cat_low(t):
                dve.wait_ge(s_ch, t + 1)
                low(catT[:, LO, t % 2], psum[:, 0:2, :].rearrange("p b (k c) -> p (b k) c", c=P), catT[:, HI, t % 2]).then_inc(s_catTc, 1)

            def layer_norm_1(t):
                dve.wait_ge(s_mix, t + 1)
                dve.wait_ge(s_xa[t % 2], 16 * (t // 2 + 1))
                r = resid[:, t % 2]
                if t >= 2:
                    dve.wait_ge(s_x1, t - 1)
                link_res(nc.vector.scalar_tensor_tensor(r, x_again[:, t % 2], ALPHA, psum[:, 2 + 2 * (t % 2):4 + 2 * (t % 2), :]
                                                        .rearrange("p b c -> p (b c)"), ALU.mult, ALU.add), t)
                dve.wait_ge(s_stat, TILES + t)
                for i in range(2):
                    ins = nc.vector.bn_stats(stats[:, i, :], r[:, i * 512:(i + 1) * 512])
                link(ins)
                nc.vector.bn_aggr(mv[:, t, :], stats).then_inc(s_stat, 1)
                dve.wait_ge(s_rstd, TILES + t + 1)
                link(nc.vector.scalar_tensor_tensor(r, r, mv[:, t, 0:1], ln1_g, ALU.subtract, ALU.mult))
                if t >= 2:
                    dve.wait_ge(s_x1st[t % 2], 32 * (t // 2))
                    dve.wait_ge(s_ax1, t - 1)
                    dve.wait_ge(s_x1T, t - 1)
                nc.vector.scalar_tensor_tensor(x1[:, t % 2], r, rstd[:, t:t + 1], ln1_b, ALU.mult, ALU.add).then_inc(s_x1, 1)

            def link_res(ins, t):
                ins.then_inc(s_res, 1)
                dve.wait_ge(s_res, t + 1)

            def soft_max(t):
                dve.wait_ge(s_log, t + 1)
                if t:
                    dve.wait_ge(s_smx, t)
                link(nc.vector.reduce_max(lmx, psum[:, 6, 0:EXPERTS], AX_X))
                nc.vector.tensor_scalar(smx[:, t % 2:t % 2 + 1], lmx, -1.0, None, ALU.mult).then_inc(s_smx, 1)

            def soft_norm(t):
                dve.wait_ge(s_sexp, t + 1)
                if t >= 2:
                    dve.wait_ge(s_affT, t - 1)
                dve.wait_ge(s_aff, t) if t else dve.wait_ge(s_att, NU)
                link(nc.vector.reciprocal(rden[:, 0:1], ssum[:, t % 2:t % 2 + 1]))
                nc.vector.tensor_scalar(aff[:, t % 2], aff_e[:, t % 2], rden[:, 0:1], None, ALU.mult).then_inc(s_aff, 1)

            def aff_copy(t):
                dve.wait_ge(s_affT, t + 1)
                dst = aff_a[32:32 + EXPERTS, t * P:(t + 1) * P] if t < PT else aff_a[0:EXPERTS, (t - PT) * P:(t - PT + 1) * P]
                nc.vector.tensor_copy(dst, psum[0:EXPERTS, 7, 0:P]).then_inc(s_affTc, 1)

            dve.wait_ge(s_ln1, 48)
            cat_low(0)
            for k in range(KT):
                dve.wait_ge(s_oh, k + 1)
                low(wout_lo[:, k, :], wout[:, k, :], wout_hi[:, k, :]).then_inc(s_ol, 1)
            dve.wait_ge(s_ol, KT)
            link(nc.vector.memset(aff_a[0:48, :], -1.0))
            for t in range(TILES + 2):
                if 2 <= t < TILES + 1:
                    aff_copy(t - 2)
                if t + 1 < TILES:
                    cat_low(t + 1)
                if t < TILES:
                    layer_norm_1(t)
                if 0 <= t - 1 < TILES:
                    soft_max(t - 1)
                    soft_norm(t - 1)
            aff_copy(TILES - 1)

            dve.wait_ge(s_affTc, TILES)
            cur, nxt = aff_a, aff_b
            for i in range(CAP_S // 8):
                v8 = top_val[0:48, 8 * i:8 * i + 8]
                link(nc.vector.max(v8, cur[0:48, :]))
                nc.vector.max_index(top_idx[0:48, 8 * i:8 * i + 8], v8, cur[0:48, :])
                link(nc.vector.match_replace(nxt[0:48, :], v8, cur[0:48, :], -1.0))
                cur, nxt = nxt, cur
            link(nc.vector.tensor_copy(top_idf[0:48, :], top_idx[0:48, :]))
            nc.vector.tensor_scalar(top_idf[0:EXPERTS, :], top_idf[0:EXPERTS, :], float(L_PROMPT), None, ALU.add).then_inc(s_top, 1)
            link(nc.vector.memset(gates, 0.0))
            link(nc.vector.memset(yT, 0.0))
            dve.wait_ge(s_topT, 1)
            for g in range(2):
                c = slice(32 * g, 32 * g + EXPERTS)
                nc.vector.tensor_copy(gates[:, g, 1:EXPERTS + 1], psum[:, 0, c])
                nc.vector.tensor_copy(idx[:, g, 0:EXPERTS], psum[:, 1, c])
                ins = nc.vector.tensor_copy(idx[:, g, EXPERTS:EXPERTS + 1], psum[:, 1, c.stop - 1:c.stop])
            ins.then_inc(s_idx, 1)
            dve.wait_ge(s_idx, 1)


            def xs_low(count):
                dve.wait_ge(s_xsH, count)
                for b in range(3):
                    nk = min(3, KT - 3 * b)
                    ks = slice(3 * b, 3 * b + nk)
                    last = low(xs_parts[:, LO, ks, :], psum[:, b, 0:nk * SLOTS].rearrange("p (k c) -> p k c", k=nk), xs_parts[:, HI, ks, :])
                last.then_inc(s_xsL, 1)

            def both(out, banks):
                return nc.vector.reduce_sum(out, banks, AX_X)

            def y_copy(half, count):
                dve.wait_ge(s_unit, count)
                for i in range(4):
                    both(yT[:, 4 * half + i, :], psum[:, 4 + i, 0:2 * SLOTS].rearrange("p (c s) -> p s c", c=2)).then_inc(s_yT, 1)

            xs_low(1)
            dve.sem_inc(s_gate, 1)
            dve.sem_inc(s_mul, 1)
            dve.sem_inc(s_hid, 1)
            with dve.Fori(0, EXPERTS) as e:
                for u in range(UNITS):
                    dve.wait_ge(s_hi, e * UNITS + (u + 1))
                    low(w_parts[:, LO, u % SPLIT, :], raw[:, u % RING, :], w_parts[:, HI, u % SPLIT, :]).then_inc(s_lo, 1)
                    if u == 4:
                        y_copy(1, e * UNITS + SPLIT)
                    if u % 4 == 2 and 6 <= u <= GU_UNITS + 2:
                        pr = (u - 6) // 4
                        dve.wait_ge(s_unit, e * UNITS + (4 * pr + 2 + SPLIT))
                        dve.wait_ge(s_silu, e * PAIRS + max(pr, 1))
                        both(gate_sum[:, pr % 2], psum[:, 0:2, 0:2 * SLOTS].rearrange("p j (c s) -> p j s c", c=2)).then_inc(s_gate, 1)
                    if u % 4 == 0 and 8 <= u <= GU_UNITS + 4:
                        pr = (u - 8) // 4
                        dve.wait_ge(s_unit, e * UNITS + (4 * pr + 4 + SPLIT))
                        dve.wait_ge(s_mul, e * PAIRS + (pr + 1))
                        both(up_sum, psum[:, 2:4, 0:2 * SLOTS].rearrange("p j (c s) -> p j s c", c=2)).then_inc(s_up, 1)
                        dve.wait_ge(s_up, e * PAIRS + (pr + 1))
                        dve.wait_ge(s_silu, e * PAIRS + (pr + 2))
                        dve.wait_ge(s_hid, e * PAIRS + max(pr, 1))
                        nc.vector.tensor_tensor(hid[:, pr % 2], sg[:, pr % 2], up_sum, ALU.mult).then_inc(s_mul, 1)
                    if u % 4 == 2 and 10 <= u <= GU_UNITS + 6:
                        pr = (u - 10) // 4
                        dve.wait_ge(s_hh, e * PAIRS + (pr + 1))
                        low(h_parts[:, LO, 2 * pr:2 * pr + 2, :], hid[:, pr % 2], h_parts[:, HI, 2 * pr:2 * pr + 2, :]).then_inc(s_hid, 1)
                    if u == GU_UNITS + 8:
                        xs_low(e + 2)
                    if u == GU_UNITS + DN_UNITS + 4:
                        y_copy(0, e * UNITS + (GU_UNITS + DN_UNITS + SPLIT))
            y_copy(1, EXPERTS * UNITS + SPLIT)

            dve.wait_ge(s_ln2, 32)
            for t in range(TILES):
                dve.wait_ge(s_fin_in[t % 5], 16 * (t // 5 + 1))
                r = fin_in[:, t % 5]
                dve.wait_ge(s_stat, 2 * TILES + t)
                for i in range(2):
                    ins = nc.vector.bn_stats(stats[:, i, :], r[:, i * 512:(i + 1) * 512])
                link(ins)
                nc.vector.bn_aggr(mv[:, t, :], stats).then_inc(s_stat, 1)
                dve.wait_ge(s_rstd, 2 * TILES + t + 1)
                link(nc.vector.scalar_tensor_tensor(r, r, mv[:, t, 0:1], ln2_g, ALU.subtract, ALU.mult))
                if t >= 5:
                    dve.wait_ge(s_out[t % 5], 16 * (t // 5))
                nc.vector.scalar_tensor_tensor(fin_out[:, t % 5], r, rstd[:, t:t + 1], ln2_b, ALU.mult, ALU.add).then_inc(s_fin, 1)

        @block.gpsimd
        def _(pool):
            chain = [0]

            def link(ins):
                chain[0] += 1
                ins.then_inc(s_pool, 1)
                pool.wait_ge(s_pool, chain[0])

            nc.gpsimd.memset(ident, 0.0).then_inc(s_ident, 1)
            link(nc.gpsimd.memset(half_neg, -0.5))
            pool.wait_ge(s_ident, 1)
            nc.gpsimd.affine_select(out=ident, in_=ident, compare_op=ALU.not_equal, fill=1.0, base=0,
                                    pattern=[[-1, P]], channel_multiplier=1).then_inc(s_ident, 1)
            def rstds(lo, hi):
                for n in range(lo, hi):
                    t = n % TILES
                    pool.wait_ge(s_stat, n + 1)
                    if n:
                        pool.wait_ge(s_rstd, n)
                    link(nc.gpsimd.tensor_scalar(veps, mv[:, t, 1:2], EPS, None, ALU.add))
                    nc.gpsimd.tensor_tensor(rstd[:, t:t + 1], veps, half_neg, ALU.pow).then_inc(s_rstd, 1)

            rstds(0, 2 * TILES)

            def gather(e, copied, count):
                nc.gpsimd.tensor_copy(idx_g, idx[:, :, bass.ds(e, 1)].rearrange("p g o -> p (g o)")).then_inc(copied, 1)
                pool.wait_ge(s_idx, 1)
                pool.wait_ge(copied, count)
                pool.indirect_dma_start(xs, None, x1_d, bass.IndirectOffsetOnAxis(ap=idx_g[:, 0:1], axis=0)).then_inc(s_gath, 16)
                pool.indirect_dma_start(xs_p[0:CAP_P, :], None, x1_d,
                                        bass.IndirectOffsetOnAxis(ap=idx_g[0:CAP_P, 1:2], axis=0)).then_inc(s_gath, 16)

            for i in range(2):
                pool.wait_ge(s_x1st[i], 32 * (TILES // 2))
            pool.wait_ge(s_idx, 1)
            gather(0, s_gi0, 1)
            pool.wait_ge(s_xsT, 1)
            gather(1, s_gi, 1)

            def scatter(e):
                pool.wait_ge(s_gi, e + 1)
                pool.wait_ge(s_ys, e * 2 + 4)
                nc.gpsimd.tensor_copy(idx_s, idx[:, :, bass.ds(e, 1)].rearrange("p g o -> p (g o)")).then_inc(s_si, 1)
                pool.wait_ge(s_idx, 1)
                pool.wait_ge(s_si, e + 1)
                pool.indirect_dma_start(acc_d, bass.IndirectOffsetOnAxis(ap=idx_s[:, 0:1], axis=0), ys, None,
                                        compute_op=ALU.add).then_inc(s_scat, 16)
                pool.indirect_dma_start(acc_d, bass.IndirectOffsetOnAxis(ap=idx_s[0:CAP_P, 1:2], axis=0), ys_p[0:CAP_P, :], None,
                                        compute_op=ALU.add).then_inc(s_scat, 16)

            with pool.Fori(0, EXPERTS - 1) as e:
                scatter(e)
                pool.wait_ge(s_scat, e * 32 + 32)
                pool.wait_ge(s_xsT, e + 2)
                gather(e + 2, s_gi, e + 2)
            scatter(EXPERTS - 1)
            rstds(2 * TILES, 3 * TILES)


NAMES = ["x_prompt", "x_sample", "rel_bias_table", "w_in", "b_in", "gmlp_ln_g", "gmlp_ln_b", "gmlp_w_s", "gmlp_b_s",
         "w_out", "ln1_g", "ln1_b", "w_router", "w_gate", "w_up", "w_down", "ln2_g", "ln2_b"]


def kernel(**inputs):
    import concourse.bacc as bacc
    from concourse.bass_utils import run_bass_kernel_spmd

    nc = bacc.Bacc("TRN2", target_bir_lowering=False, num_devices=1)
    arrays, aps = {}, {}
    for name in NAMES + ["rel_rows"]:
        x = relative_rows() if name == "rel_rows" else np.ascontiguousarray(inputs[name])
        arrays["in_" + name] = x
        aps[name] = nc.dram_tensor("in_" + name, x.shape, mybir.dt.from_np(x.dtype), kind="ExternalInput").ap()
    outs = [nc.dram_tensor(n, (1, length, D), F32, kind="ExternalOutput").ap()
            for n, length in (("y_prompt", L_PROMPT), ("y_sample", L_SAMPLE))]
    build(nc, aps, outs)
    r = run_bass_kernel_spmd(nc, [arrays], core_ids=[0]).results[0]
    return r["y_prompt"], r["y_sample"]
```

```python
import math
from contextlib import ExitStack

import numpy as np
import concourse.bass as bass
from concourse import mybir

F32 = mybir.dt.float32
F32R = mybir.dt.float32r
U32 = mybir.dt.uint32
ALU = mybir.AluOpType
ACT = mybir.ActivationFunctionType
AX_X = mybir.AxisListType.X

P = 128
D = 1024
KT = D // P
L_PROMPT, L_SAMPLE = 256, 1024
TOKENS = L_PROMPT + L_SAMPLE
TILES = TOKENS // P
PT = L_PROMPT // P
HEADS, HD = 8, 64
AW = HEADS * HD
E_IN = 5 * AW
EXPERTS, FF = 16, 2816
FT = FF // P
CAP_P, CAP_S = 2 * L_PROMPT // EXPERTS, 2 * L_SAMPLE // EXPERTS
SLOTS = CAP_S + CAP_P
ALPHA = 2.0 ** 0.25
EPS = 1e-5
N_BUCKETS, MAX_DIST = 32, 1024
REL = 2 * L_SAMPLE
BIAS_W = L_SAMPLE - P + L_SAMPLE
MASKED = -1e30

PAIRS = FT // 2
GU_UNITS = 4 * PAIRS
DN_UNITS = PAIRS
UNITS = GU_UNITS + 2 * DN_UNITS
RING = 11
SPLIT = 6
W_COLS = 256
UW = 1024


def relative_rows():
    rel = (L_SAMPLE - 1) - np.arange(REL)
    half = N_BUCKETS // 2
    n = np.abs(rel)
    max_exact = half // 2
    large = max_exact + (np.log(np.maximum(n, 1) / max_exact) / np.log(MAX_DIST / max_exact)
                         * (half - max_exact)).astype(np.int32)
    bucket = np.where(rel > 0, half, 0) + np.where(n < max_exact, n, np.minimum(large, half - 1))
    count = sum(((n <= w // 2) & (n % d == 0)).astype(np.int64) for w, d in ((128, 1), (512, 4), (2048, 16)))
    rows = np.zeros((N_BUCKETS + 1, REL), np.float32)
    rows[bucket, np.arange(REL)] = 1.0
    rows[N_BUCKETS] = np.where(count > 0, np.log(np.maximum(count, 1)), MASKED)
    return rows


def build(nc, a, outs):
    out_prompt, out_sample = outs
    w_in, w_out = a["w_in"][0], a["w_out"][0]
    w_gate, w_up, w_down = a["w_gate"][0], a["w_up"][0], a["w_down"][0]
    x1_d = nc.dram_tensor("x1_rows", (TOKENS, D), F32, kind="Internal").ap()
    acc_d = nc.dram_tensor("acc_rows", (TOKENS, D), F32, kind="Internal").ap()
    rel_d = nc.dram_tensor("rel_bias", (HEADS, REL), F32, kind="Internal").ap()

    def token_rows(prompt, sample, t):
        return prompt[0, t * P:(t + 1) * P, :] if t < PT else sample[0, (t - PT) * P:(t - PT + 1) * P, :]

    with ExitStack() as ctx:
        def sem(name):
            return ctx.enter_context(nc.semaphore(name))

        psum = ctx.enter_context(nc.psum_tensor("banks", [P, 8, 512], F32))
        HI, LO = 0, 1

        def place(name, start, *shape, dt=F32):
            with ExitStack() as alone:
                if start:
                    alone.enter_context(nc.sbuf_tensor(name + "_below", [P, start], F32))
                return alone.enter_context(nc.sbuf_tensor(name, [P, *shape], dt))[(slice(None),) * (1 + len(shape))]

        x_parts = place("x_parts", 0, 2, KT, TOKENS, dt=F32R)
        win_parts = place("win_parts", 20480, 2, 2, KT, W_COLS, dt=F32R)
        win_raw = place("win_raw", 28672, 2, KT, W_COLS)
        qT_last = place("qT_last", 28672, 1, TOKENS)
        x_rows = place("x_rows", 32768, TILES, D)
        gm = place("gm", 32768, TILES, AW)
        v_rows = place("v_rows", 37888, TILES, AW)
        wsT = place("wsT", 37888, 2, 4, P)
        pre_t = place("pre_gelu", 38912, 2, 2 * W_COLS)
        pre = [pre_t[:, 0, :], pre_t[:, 1, :]]
        qT_first = place("qT_first", 43008, 3, TOKENS)
        rowb = place("uv_bias", 43008, 2, AW)
        gln = place("gmlp_ln", 44032, 2, AW)
        ws_rows = place("ws_rows", 45056, 8, P)
        kT = place("kT", 46848, 4, TOKENS)
        vn = place("vn", 46848, TILES, AW)
        rel_rows = place("rel_rows", 46848, REL)
        rel_bias = place("rel_table", 48896, REL)
        gln_g, gln_b = gln[:, 0, :], gln[:, 1, :]

        def q_tile(et):
            return qT_first[:, et, :] if et < 3 else qT_last[:, 0, :]

        relT = place("relT", 0, 2, BIAS_W)
        scored = place("scored", 3840, 2, L_SAMPLE)
        probs = place("probs", 5888, 3, L_SAMPLE)
        probsT = place("probsT", 8960, 2, KT, P)
        q_parts = place("q_parts", 11008, 2, TOKENS, dt=F32R)
        k_high = place("k_high", 13568, 2, TOKENS, dt=F32R)
        k_low = place("k_low", 16128, 2, TOKENS, dt=F32R)
        wout = place("wout_raw", 43008, KT, D)
        att = place("att", 20480, TILES, AW)
        ln1 = place("ln1", 25600, 2, D)
        ln1_g, ln1_b = ln1[:, 0, :], ln1[:, 1, :]
        wr = place("w_router", 27648, KT, EXPERTS)
        x_again = place("x_again", 16384, 2, D)
        wout_hi = place("wout_hi", 0, KT, D, dt=F32R)
        wout_lo = place("wout_lo", 37888, KT, D, dt=F32R)
        catT = place("catT_parts", 28672, 2, 2, KT, P, dt=F32R)
        ax1 = place("ax1", 8192, 2, D)
        resid = place("resid", 10240, 2, D)
        x1 = place("x1", 12288, 2, D)
        x1T = place("x1T", 14336, 2, KT, P)
        aff_a = place("aff_rows", 18432, L_SAMPLE)
        aff_b = place("aff_rows_next", 16384, L_SAMPLE)
        top = place("top", 19456, 3, CAP_S)
        top_val, top_idx, top_idf = top[:, 0, :], top[:, 1, :].bitcast(U32), top[:, 2, :]
        aff = place("aff", 19840, 2, EXPERTS)
        aff_e = place("aff_exp", 19872, 2, EXPERTS)
        gates = place("gates", 19904, 2, EXPERTS + 1)
        idx = place("idx", 19952, 2, EXPERTS + 1)[:, :, :].bitcast(U32)
        idx_g = place("idx_gather", 20000, 2)[:, :].bitcast(U32)
        idx_s = place("idx_scatter", 20016, 2)[:, :].bitcast(U32)
        sm = place("softmax_small", 20032, 4)
        smx, ssum = sm[:, 0:2], sm[:, 2:4]
        raw = place("raw_units", 0, RING, UW)
        ln2 = place("ln2", 11264, 2, D)
        ln2_g, ln2_b = ln2[:, 0, :], ln2[:, 1, :]
        w_parts = place("w_parts", 20480, 2, SPLIT, UW, dt=F32R)
        xs_parts = place("xs_parts", 32768, 2, KT, SLOTS, dt=F32R)
        h_parts = place("h_parts", 35328, 2, FT, SLOTS, dt=F32R)
        xs = place("xs", 42368, D)
        xs_p = place("xs_prompt", 43392, D)
        hid = place("hidden", 44416, 2, 2, SLOTS)
        sg = place("silu_gate", 45056, 2, 2, SLOTS)
        gate_sum = place("gate_sum", 45696, 2, 2, SLOTS)
        up_sum = place("up_sum", 46336, 2, SLOTS)
        yT = place("yT", 46656, KT, SLOTS)
        ys = place("ys", 47936, D)
        ys_p = place("ys_prompt", 48960, D)
        last_idx = place("last_idx", 20048, 2)
        numbers = place("token_numbers", 13312, TOKENS)
        sel = place("last_selection", 14592, TOKENS, dt=F32R)
        acc = place("acc_tiles", 0, TILES, D)
        fin = place("fin", 20480, 5, D)
        ys_parts = place("ys_parts", 26624, 2, 2, D, dt=F32R)
        nmr = place("minus_mean_rstd", 52832, TILES)
        fin_stats = place("fin_stats", 25600, 2, 2, 6)
        v_bias = place("v_bias", 51968, AW)
        ident = place("ident", 52480, P)
        table = place("table", 52608, HEADS)
        b_qk = place("b_qk", 52624, 8)
        b_s = place("b_s", 52640, 8)
        half_neg = place("half_neg", 52656, 1)
        veps = place("veps", 52672, 1)
        rstd = place("rstd", 52688, TILES)
        mv = place("mv", 52704, TILES, 2)
        stats = place("stats", 52736, 2, 6)
        mx = place("mx", 52752, 4)
        nmx = place("nmx", 52768, 4)
        den = place("den", 52784, 8)
        rden = place("rden", 52800, 2)
        lmx = place("lmx", 52816, 1)

        s_const, s_rel_in, s_bs, s_rows = sem("const_in"), sem("rel_in"), sem("small_in"), sem("rows_in")
        s_x = [sem(f"x_in{t}") for t in range(TILES)]
        s_win = [sem(f"win_in{i}") for i in range(2)]
        s_wh, s_wl, s_xh = sem("win_high"), sem("win_low"), sem("x_high")
        s_oh, s_ol, s_ch = sem("wout_high"), sem("wout_low"), sem("catT_high")
        s_ident, s_table1 = sem("ident_ready"), sem("table_one")
        s_job = sem("job_done")
        s_free = {"act": sem("freed_by_act"), "dve": sem("freed_by_dve")}
        s_rel_out, s_relT = sem("rel_stored"), [sem(f"relT_in{i}") for i in range(2)]
        s_gelu = sem("gelu_done")
        s_stat, s_rstd, s_vn = sem("stats_done"), sem("rstd_ready"), sem("vn_ready")
        s_pool = sem("pool_chain")
        s_dch = sem("dve_chain")
        s_bq = sem("bq_scaled")
        s_qk, s_scored, s_probs = sem("qk_done"), sem("scored"), sem("probs_ready")
        s_pt, s_ptc, s_pv, s_att = sem("probsT_done"), sem("probsT_copied"), sem("pv_done"), sem("att_out")
        s_wout, s_ln1, s_xa = sem("wout_in"), sem("ln1_in"), [sem(f"x_again{i}") for i in range(2)]
        s_sh, s_sl = sem("qk_high"), sem("qk_low")
        s_catT, s_catTc, s_mix = sem("catT_done"), sem("catT_copied"), sem("mix_done")
        s_res = sem("resid_done")
        s_x1, s_ax1, s_x1st = sem("x1_ready"), sem("ax1_ready"), [sem(f"x1_stored{i}") for i in range(2)]
        s_x1T, s_x1Tc, s_log = sem("x1T_done"), sem("x1T_copied"), sem("logits_done")
        s_smx, s_sexp, s_aff, s_affT, s_affTc = (sem("logit_max"), sem("logit_exp"), sem("aff_ready"),
                                                 sem("affT_done"), sem("affT_copied"))
        s_top, s_topT, s_idx = sem("top_ready"), sem("topT_done"), sem("idx_ready")
        s_unit_in = [sem(f"unit_in{i}") for i in range(RING)]
        s_unit = sem("units_done")
        s_hi, s_lo = sem("unit_high"), sem("unit_low")
        s_gate, s_up = sem("gate_summed"), sem("up_summed")
        s_silu, s_mul, s_hh, s_hid = sem("silu_done"), sem("hidden_done"), sem("hidden_high"), sem("hidden_low")
        s_gath = sem("gathered")
        s_xsT, s_xsH, s_xsL = sem("xsT_done"), sem("xs_high"), sem("xs_low")
        s_yT, s_yt, s_ys = sem("yT_copied"), sem("y_transposed"), sem("ys_ready")
        s_scat, s_gi0, s_gi, s_si = sem("scattered"), sem("first_idx"), sem("gather_idx"), sem("scatter_idx")
        s_acc = [sem(f"acc_in{i}") for i in range(TILES)]
        s_numbers, s_sel = sem("numbers_in"), sem("selection_ready")
        s_yh, s_yl = sem("ys_high"), sem("ys_low")
        s_sum, s_fst, s_frs = sem("rows_summed"), sem("fin_stats_done"), sem("fin_rstd")
        s_norm, s_gain = sem("normalised"), sem("gain_applied")
        s_ln2, s_fin, s_out = sem("ln2_in"), sem("fin_ready"), [sem(f"out_stored{i}") for i in range(5)]

        jobs = [("rel", i, "dve") for i in range(4)]
        jobs += [("xT", (t, i), "dve") for t in range(TILES) for i in range(2)]
        jobs += [("ws", i, "act") for i in range(2)]
        CH = [(0, 512), (512, 512), (1024, 256)]
        BLOCKS = [("gv", 4 * AW), ("gu", 3 * AW), ("v", 2 * AW), ("k", AW), ("q", 0)]
        WUNITS = [(name, half, c + half * W_COLS) for name, c in BLOCKS for half in range(AW // W_COLS)]
        for name, half, _ in WUNITS:
            if (name, half) == ("v", 0):
                jobs += [("gm", t, "dve") for t in range(TILES)]
            if name in ("q", "k"):
                jobs += [(name, (2 * half + j, c), "act") for j in range(2) for c in range(3)]
            else:
                jobs += [(name, (half, t), "dve") for t in range(TILES)]
        freed = []
        for n, (_, _, eng) in enumerate(jobs):
            freed.append(1 + sum(e == eng for _, _, e in jobs[:n]))

        unit_jobs = [1 + max(n for n, j in enumerate(jobs) if j[0] == name and
                             (j[1][0] // 2 == half if name in ("q", "k") else j[1][0] == half))
                     for name, half, _ in WUNITS]

        units = [(h, g, qt) for h in range(HEADS) for g in range(2)
                 for qt in range(PT if g == 0 else TILES - PT)]
        NU = len(units)
        glen = (L_PROMPT, L_SAMPLE)
        HU = NU // HEADS
        PIECES = [(0, L_PROMPT), (L_PROMPT, L_SAMPLE)]
        HIGH_STEPS = [(what, piece) for piece in range(2) for what in ("k again", "q", "k")]
        LOW_STEPS = [(what, piece) for piece in range(2) for what in ("q", "k")]
        FIN_ORDER = [*range(PT, TILES), *range(PT)]
        FIN_BANKS = (0, 2, 6, 4)
        gtile = (0, PT)

        block = ctx.enter_context(nc.Block())

        def unit_src(e, u):
            if u < GU_UNITS:
                pr, kind = u // 4, u % 4
                w = (w_gate, w_up)[kind // 2]
                k0 = (kind % 2) * (KT // 2) * P
                return w[e, k0:k0 + KT // 2 * P, pr * 2 * P:(pr + 1) * 2 * P].rearrange("(k p) f -> p k f", p=P)
            half, pr = divmod(u - GU_UNITS, DN_UNITS)
            return w_down[e, pr * 2 * P:(pr + 1) * 2 * P, half * 512:(half + 1) * 512].rearrange("(k p) f -> p k f", p=P)

        def unit_dst(u):
            k = KT // 2 if u % UNITS < GU_UNITS else 2
            return raw[:, u % RING, :].rearrange("p (k f) -> p k f", k=k)

        @block.sync
        def _(sp):
            def load_win(n):
                if n >= 2:
                    sp.wait_ge(s_wl, n - 1)
                c = WUNITS[n][2]
                sp.dma_start(win_raw[:, n % 2], w_in[:, c:c + W_COLS].rearrange("(k p) f -> p k f", p=P)).then_inc(s_win[n % 2], 16)

            for t in range(TILES):
                sp.dma_start(x_rows[:, t], token_rows(a["x_prompt"], a["x_sample"], t)).then_inc(s_x[t], 16)
                if t in (3, 7):
                    load_win(t // 4)
            sp.wait_ge(s_free["dve"], 4)
            sp.dma_start(rel_d[:, :], rel_bias[0:HEADS, :]).then_inc(s_rel_out, 16)
            for n in range(2, len(WUNITS)):
                load_win(n)
            sp.wait_ge(s_job, len(jobs))
            sp.wait_ge(s_rel_out, 16)

            def load_relT(h):
                if h >= 2:
                    sp.wait_ge(s_scored, 10 * (h - 1))
                src = bass.AP(tensor=rel_d.tensor, offset=h * REL, ap=[[1, P], [1, BIAS_W]])
                sp.dma_start(relT[:, h % 2, :], src).then_inc(s_relT[h % 2], 16)

            load_relT(0)
            load_relT(1)
            for i, name in enumerate(("ln1_g", "ln1_b")):
                sp.dma_start(ln1[:, i, :], a[name][0:1, :].to_broadcast([P, D])).then_inc(s_ln1, 16)
            sp.dma_start(wr, a["w_router"][0].rearrange("(k p) e -> p k e", p=P)).then_inc(s_ln1, 16)

            def load_x(t):
                if t >= 2:
                    sp.wait_ge(s_res, t - 1)
                sp.dma_start(x_again[:, t % 2], token_rows(a["x_prompt"], a["x_sample"], t)).then_inc(s_xa[t % 2], 16)

            for h in range(2, HEADS):
                load_relT(h)
            sp.wait_ge(s_sl, len(LOW_STEPS) * HEADS)
            sp.dma_start(wout[:, :, :], w_out.rearrange("(k p) f -> p k f", p=P)).then_inc(s_wout, 16)
            sp.wait_ge(s_qk, NU)
            load_x(0)
            load_x(1)
            for t in range(TILES):
                if t + 2 < TILES:
                    load_x(t + 2)
                sp.wait_ge(s_x1, t + 1)
                sp.dma_start(x1_d[t * P:(t + 1) * P, :], x1[:, t % 2]).then_inc(s_x1st[t % 2], 16)
                sp.wait_ge(s_ax1, t + 1)
                sp.dma_start(acc_d[t * P:(t + 1) * P, :], ax1[:, t % 2]).then_inc(s_x1st[t % 2], 16)
            for i in range(2):
                sp.wait_ge(s_x1st[i], 32 * (TILES // 2))
            for u in range(RING):
                sp.dma_start(unit_dst(u), unit_src(0, u)).then_inc(s_unit_in[u], 16)
            sp.wait_ge(s_x1T, TILES)
            for i, name in enumerate(("ln2_g", "ln2_b")):
                sp.dma_start(ln2[:, i, :], a[name][0:1, :].to_broadcast([P, D])).then_inc(s_ln2, 16)
            sp.dma_start(numbers, a["token_numbers"].to_broadcast([P, TOKENS])).then_inc(s_numbers, 16)

            with sp.Fori(0, EXPERTS - 1) as e:
                for u in range(UNITS):
                    n = u + RING
                    if n % UNITS not in (0, 2, GU_UNITS):
                        sp.wait_ge(s_lo, e * UNITS + (u + 1 + ((n + 1) % UNITS in (0, 2, GU_UNITS))))
                    sp.dma_start(unit_dst(n), unit_src(e + n // UNITS, n % UNITS)).then_inc(s_unit_in[n % RING], 16)
            for u in range(UNITS - RING):
                n = u + RING
                sp.wait_ge(s_lo, (EXPERTS - 1) * UNITS + u + 1)
                sp.dma_start(unit_dst(n), unit_src(EXPERTS - 1, n)).then_inc(s_unit_in[n % RING], 16)

            sp.wait_ge(s_scat, 32 * (EXPERTS - 1))
            for i, t in enumerate(FIN_ORDER):
                sp.wait_ge(s_lo, (EXPERTS - 1) * UNITS + (UNITS - RING + i + 1))
                sp.dma_start(acc[:, i, :], acc_d[t * P:(t + 1) * P, :]).then_inc(s_acc[i], 16)
            for i, t in enumerate(FIN_ORDER):
                sp.wait_ge(s_fin, i + 1)
                sp.dma_start(token_rows(out_prompt, out_sample, t), fin[:, i % 5]).then_inc(s_out[i % 5], 16)
            for i in range(5):
                sp.wait_ge(s_out[i], 16 * (TILES // 5))

        @block.tensor
        def _(pe):
            pe.wait_ge(s_ident, 2)
            jn = [0]
            waited = {"act": 0, "dve": 0}

            def job(name):
                n = jn[0]
                assert jobs[n][0] == name
                if n >= 8:
                    eng, c = jobs[n - 8][2], freed[n - 8]
                    if c > waited[eng]:
                        pe.wait_ge(s_free[eng], c)
                        waited[eng] = c
                jn[0] += 1
                return psum[:, n % 8, :], jobs[n][1]

            pe.wait_ge(s_rel_in, 32)
            pe.wait_ge(s_table1, 1)
            for i in range(4):
                bank, _ = job("rel")
                nc.tensor.matmul(bank[0:HEADS, :], table[0:N_BUCKETS + 1, :], rel_rows[0:N_BUCKETS + 1, i * 512:(i + 1) * 512],
                                 start=True, stop=True).then_inc(s_job, 1)
            for t in range(TILES):
                pe.wait_ge(s_x[t], 16)
                for i in range(2):
                    bank, _ = job("xT")
                    for k in range(4):
                        last = nc.tensor.transpose(bank[:, k * P:(k + 1) * P], x_rows[:, t, (4 * i + k) * P:(4 * i + k + 1) * P], ident)
                    last.then_inc(s_job, 1)
            pe.wait_ge(s_rows, 16)
            for i in range(2):
                bank, _ = job("ws")
                for g in range(4):
                    last = nc.tensor.transpose(bank[:, g * P:(g + 1) * P], ws_rows[:, 4 * i + g, :], ident)
                last.then_inc(s_job, 1)
            pe.wait_ge(s_free["dve"], freed[3 + 2 * TILES])

            def three_parts(out, w_of, x_of, first, last_one):
                for n, (wp, xp) in enumerate(((HI, HI), (HI, LO), (LO, HI))):
                    last = nc.tensor.matmul(out, w_of(wp), x_of(xp), start=first and n == 0, stop=last_one and n == 2)
                return last

            for u, (name, half, _) in enumerate(WUNITS):
                if (name, half) == ("v", 0):
                    for t in range(TILES):
                        bank, _ = job("gm")
                        pe.wait_ge(s_vn, t + 1)
                        for g in range(8):
                            last = nc.tensor.matmul(bank[:, g * HD:(g + 1) * HD], wsT[:, g // 4, g % 4, :],
                                                    vn[:, t, g * HD:(g + 1) * HD], start=True, stop=True)
                        last.then_inc(s_job, 1)
                pe.wait_ge(s_wl, u + 1)
                w = win_parts[:, :, u % 2]
                if name in ("q", "k"):
                    for j in range(2):
                        for c0, cn in CH:
                            bank, _ = job(name)
                            for k in range(KT):
                                last = three_parts(bank[:, 0:cn], lambda p: w[:, p, k, j * P:(j + 1) * P],
                                                   lambda p: x_parts[:, p, k, c0:c0 + cn], k == 0, k == KT - 1)
                            last.then_inc(s_job, 1)
                else:
                    for t in range(TILES):
                        bank, _ = job(name)
                        for k in range(KT):
                            last = three_parts(bank[:, 0:W_COLS], lambda p: x_parts[:, p, k, t * P:(t + 1) * P],
                                               lambda p: w[:, p, k, :], k == 0, k == KT - 1)
                        last.then_inc(s_job, 1)

            for eng in ("act", "dve"):
                pe.wait_ge(s_free[eng], sum(e == eng for _, _, e in jobs))
            for n in range(NU + 3):
                if n < NU:
                    h, g, qt = units[n]
                    if n >= 2:
                        pe.wait_ge(s_scored, n - 1)
                    if qt == 0:
                        pe.wait_ge(s_sl, len(LOW_STEPS) * h + 2 * (g + 1))
                    base, t0 = HD * (h % 2), gtile[g] * P
                    q = q_parts[:, h % 2, t0 + qt * P:t0 + (qt + 1) * P]
                    for c in range(0, glen[g], 512):
                        cn = min(512, glen[g])
                        out, ks = psum[:, 2 * (n % 2) + c // 512, 0:cn], slice(t0 + c, t0 + c + cn)
                        nc.tensor.matmul(out, q, k_high[:, h % 2, ks], start=True, stop=False)
                        last = nc.tensor.matmul(out, q[base:base + HD], k_low[base:base + HD, h % 2, ks], start=False, stop=True)
                    last.then_inc(s_qk, 1)
                if 0 <= n - 2 < NU:
                    m = n - 2
                    pe.wait_ge(s_probs, m + 1)
                    if m >= 1:
                        pe.wait_ge(s_ptc, m)
                    for kt in range(glen[units[m][1]] // P):
                        last = nc.tensor.transpose(psum[:, 4 + kt // 4, kt % 4 * P:(kt % 4 + 1) * P],
                                                   probs[:, m % 3, kt * P:(kt + 1) * P], ident)
                    last.then_inc(s_pt, 1)
                if 0 <= n - 3 < NU:
                    m = n - 3
                    h, g, qt = units[m]
                    pe.wait_ge(s_ptc, m + 1)
                    if m >= 2:
                        pe.wait_ge(s_att, m - 1)
                    nk = glen[g] // P
                    for kt in range(nk):
                        last = nc.tensor.matmul(psum[:, 6 + m % 2, 0:HD], probsT[:, m % 2, kt, :],
                                                v_rows[:, gtile[g] + kt, h * HD:(h + 1) * HD],
                                                start=kt == 0, stop=kt == nk - 1)
                    last.then_inc(s_pv, 1)

            pe.wait_ge(s_att, NU)
            pe.wait_ge(s_ln1, 48)

            def cat_transposes(t):
                if t >= 1:
                    pe.wait_ge(s_catTc, t)
                for k in range(KT):
                    src = (att if k < KT // 2 else gm)[:, t, k % (KT // 2) * P:(k % (KT // 2) + 1) * P]
                    last = nc.tensor.transpose(psum[:, k // 4, k % 4 * P:(k % 4 + 1) * P], src, ident)
                last.then_inc(s_catT, 1)

            def mix(t, j):
                if j == 0:
                    pe.wait_ge(s_catTc, t + 1)
                    if t >= 2:
                        pe.wait_ge(s_res, t - 1)
                for k in range(KT):
                    if t == 0 and j == 0:
                        pe.wait_ge(s_ol, k + 1)
                    last = three_parts(psum[:, 2 + 2 * (t % 2) + j, :], lambda p: catT[:, p, t % 2, k, :],
                                       lambda p: (wout_hi, wout_lo)[p][:, k, j * 512:(j + 1) * 512], k == 0, k == KT - 1)
                if j == 1:
                    last.then_inc(s_mix, 1)

            def x1_transposes(t):
                pe.wait_ge(s_x1, t + 1)
                if t >= 1:
                    pe.wait_ge(s_smx, t)
                    pe.wait_ge(s_sexp, t)
                    pe.wait_ge(s_affTc, t)
                for k in range(KT):
                    last = nc.tensor.transpose(psum[:, 6 + k // 4, k % 4 * P:(k % 4 + 1) * P], x1[:, t % 2, k * P:(k + 1) * P], ident)
                last.then_inc(s_x1T, 1)

            def logits(t):
                pe.wait_ge(s_x1Tc, t + 1)
                for k in range(KT):
                    last = nc.tensor.matmul(psum[:, 6, 0:EXPERTS], x1T[:, t % 2, k, :], wr[:, k, :], start=k == 0, stop=k == KT - 1)
                last.then_inc(s_log, 1)

            def aff_transpose(t):
                pe.wait_ge(s_aff, t + 1)
                if t >= 1:
                    pe.wait_ge(s_affTc, t)
                nc.tensor.transpose(psum[0:EXPERTS, 7, 0:P], aff[:, t % 2, :], ident).then_inc(s_affT, 1)

            cat_transposes(0)
            for t in range(TILES + 1):
                if t < TILES:
                    mix(t, 0)
                if t >= 2:
                    aff_transpose(t - 2)
                if t >= 1:
                    x1_transposes(t - 1)
                if t + 1 < TILES:
                    cat_transposes(t + 1)
                if t < TILES:
                    mix(t, 1)
                if t >= 1:
                    logits(t - 1)
            aff_transpose(TILES - 1)

            pe.wait_ge(s_top, 1)
            nc.tensor.transpose(psum[:, 0, 0:48], top_val[0:48, :], ident[0:48, 0:48])
            nc.tensor.transpose(psum[:, 1, 0:48], top_idf[0:48, :], ident[0:48, 0:48]).then_inc(s_topT, 1)

            def xs_transposes():
                for k in range(KT):
                    o0 = k % 3 * SLOTS
                    nc.tensor.transpose(psum[:, k // 3, o0:o0 + CAP_S], xs[:, k * P:(k + 1) * P], ident)
                    last = nc.tensor.transpose(psum[:, k // 3, o0 + CAP_S:o0 + SLOTS], xs_p[0:CAP_P, k * P:(k + 1) * P],
                                               ident[0:CAP_P, 0:CAP_P])
                last.then_inc(s_xsT, 1)

            def y_transposes(half, bank_s, bank_p):
                for i in range(4):
                    nc.tensor.transpose(psum[:, bank_s, i * P:(i + 1) * P], yT[:, 4 * half + i, 0:CAP_S], ident)
                    last = nc.tensor.transpose(psum[0:CAP_P, bank_p, i * P:(i + 1) * P], yT[:, 4 * half + i, CAP_S:SLOTS], ident)
                last.then_inc(s_yt, 1)

            pe.wait_ge(s_idx, 1)
            pe.wait_ge(s_gath, 32)
            xs_transposes()
            def product(bank, u, cols, moving, first, last_one):
                nc.tensor.matmul(bank[:, 0:2 * SLOTS], w_parts[:, HI, u % SPLIT, cols], moving(slice(HI, LO + 1)),
                                 start=first, stop=False)
                return nc.tensor.matmul(bank[:, 0:SLOTS], w_parts[:, LO, u % SPLIT, cols], moving(HI), start=False, stop=last_one)

            pe.sem_inc(s_unit, SPLIT)
            with pe.Fori(0, EXPERTS) as e:
                pe.wait_ge(s_xsL, e + 1)
                pe.wait_ge(s_ys, e * 2 + 1)
                for pr in range(PAIRS):
                    for kind in range(4):
                        u = 4 * pr + kind
                        pe.wait_ge(s_lo, e * UNITS + (u + 1))
                        if kind == 0:
                            pe.wait_ge(s_gate, e * PAIRS + (pr + 1))
                        if kind == 2:
                            pe.wait_ge(s_mul, e * PAIRS + (pr + 1))
                        for j in range(2):
                            for k in range(KT // 2):
                                kk = kind % 2 * (KT // 2) + k
                                last = product(psum[:, 2 * (kind // 2) + j, :], u, slice((2 * k + j) * P, (2 * k + j + 1) * P),
                                               lambda part, kk=kk: xs_parts[:, part, kk, :], kk == 0, kk == KT - 1)
                        last.then_inc(s_unit, 1)
                    if pr == 1:
                        pe.wait_ge(s_yT, e * 8 + 4)
                        y_transposes(1, 4, 5)
                for half in range(2):
                    for pr in range(PAIRS):
                        u = GU_UNITS + DN_UNITS * half + pr
                        pe.wait_ge(s_lo, e * UNITS + (u + 1))
                        if half == 0:
                            pe.wait_ge(s_hid, e * PAIRS + (pr + 2))
                            if pr == 0:
                                pe.wait_ge(s_ys, e * 2 + 2)
                        order = [(j, i) for j in range(2) for i in range(4)] if pr < PAIRS - 1 else \
                                [(j, i) for i in range(4) for j in range(2)]
                        for j, i in order:
                            if pr == 0 and half == 1 and j == 0:
                                pe.wait_ge(s_yT, e * 8 + (5 + i))
                            last = product(psum[:, 4 + i, :], u, slice((4 * j + i) * P, (4 * j + i + 1) * P),
                                           lambda part, f=2 * pr + j: h_parts[:, part, f, :],
                                           pr == 0 and j == 0, pr == PAIRS - 1 and j == 1)
                        last.then_inc(s_unit, 1)
                        if half == 0 and pr == 1:
                            pe.wait_ge(s_mul, e * PAIRS + (PAIRS + 1))
                            pe.wait_ge(s_gath, e * 32 + 64)
                            xs_transposes()
                        if half == 1 and pr == 2:
                            pe.wait_ge(s_xsL, e + 2)
                            pe.wait_ge(s_yT, e * 8 + 8)
                            y_transposes(0, 3, 0)

            def rows_in(i):
                pe.wait_ge(s_acc[i], 16)
                if i >= 4:
                    pe.wait_ge(s_norm, i - 3)
                for j in range(2):
                    nc.tensor.matmul(psum[:, FIN_BANKS[i % 4] + j, :], ident, acc[:, i, j * 512:(j + 1) * 512], start=True, stop=False)

            def add_last(i):
                t = FIN_ORDER[i]
                g, n = (0, CAP_S) if t >= PT else (1, CAP_P)
                pe.wait_ge(s_yl, 2 * (g + 1))
                for j in range(2):
                    for part in (HI, LO):
                        last = nc.tensor.matmul(psum[:, FIN_BANKS[i % 4] + j, :], sel[0:n, t * P:(t + 1) * P],
                                                ys_parts[0:n, part, g, j * 512:(j + 1) * 512], start=False, stop=part == LO)
                last.then_inc(s_sum, 1)

            pe.wait_ge(s_ys, EXPERTS * 2 + 1)
            rows_in(0)
            rows_in(1)
            pe.wait_ge(s_yT, EXPERTS * 8 + 4)
            y_transposes(1, 4, 5)
            rows_in(2)
            for i in range(TILES):
                add_last(i)
                if i == 0:
                    pe.wait_ge(s_ys, EXPERTS * 2 + 2)
                if i + 3 < TILES:
                    rows_in(i + 3)

        @block.scalar
        def _(act):
            act.dma_start(rel_rows[0:N_BUCKETS + 1, :], a["rel_rows"]).then_inc(s_rel_in, 16)
            act.dma_start(table[0:N_BUCKETS, :], a["rel_bias_table"]).then_inc(s_rel_in, 16)
            act.dma_start(ws_rows, a["gmlp_w_s"][0].rearrange("g p q -> p g q")).then_inc(s_rows, 16)
            act.dma_start(v_bias, a["b_in"][0:1, 2 * AW:3 * AW].to_broadcast([P, AW])).then_inc(s_const, 16)
            act.dma_start(rowb, a["b_in"][0:1, 3 * AW:5 * AW].to_broadcast([P, 2 * AW])
                          .rearrange("p (a b) -> p a b", a=2)).then_inc(s_const, 16)
            act.dma_start(gln_g, a["gmlp_ln_g"][0:1, :].to_broadcast([P, AW])).then_inc(s_const, 16)
            act.dma_start(gln_b, a["gmlp_ln_b"][0:1, :].to_broadcast([P, AW])).then_inc(s_const, 16)
            act.dma_start(b_qk, a["b_in"][0, 0:2 * AW].rearrange("(e p) -> p e", p=P),
                          allow_slow_non_contiguous=True).then_inc(s_bs, 16)
            act.dma_start(b_s, a["gmlp_b_s"][0].rearrange("g p -> p g"),
                          allow_slow_non_contiguous=True).then_inc(s_bs, 16)
            act.wait_ge(s_bs, 32)
            nc.scalar.mul(b_qk[:, 0:4], b_qk[:, 0:4], HD ** -0.5).then_inc(s_bq, 1)

            def split_win(u):
                act.wait_ge(s_win[u % 2], 16 * (u // 2 + 1))
                if u >= 2:
                    act.wait_ge(s_job, unit_jobs[u - 2])
                nc.scalar.copy(win_parts[:, HI, u % 2], win_raw[:, u % 2]).then_inc(s_wh, 1)

            gel, unit = 0, 0
            for n, (name, arg, eng) in enumerate(jobs):
                if name == "xT":
                    t, i = arg
                    act.wait_ge(s_job, n + 1)
                    nc.scalar.copy(x_parts[:, HI, 4 * i:4 * i + 4, t * P:(t + 1) * P],
                                   psum[:, n % 8, :].rearrange("p (k c) -> p k c", k=4)).then_inc(s_xh, 1)
                    if arg == (TILES - 1, 1):
                        split_win(0)
                        split_win(1)
                        unit = 2
                    continue
                if unit >= 2 and unit < len(WUNITS) and n == unit_jobs[unit - 2] + 1:
                    split_win(unit)
                    unit += 1
                if name in ("gv", "gu"):
                    half, t = arg
                    act.wait_ge(s_free["dve"], freed[n])
                    dst = (vn if name == "gv" else gm)[:, t, half * W_COLS:(half + 1) * W_COLS]
                    if gel == 0:
                        act.wait_ge(s_rel_out, 16)
                    nc.scalar.activation(dst, pre[gel % 2][:, 0:W_COLS], ACT.Gelu_apprx_tanh).then_inc(s_gelu, 1)
                    gel += 1
                if eng != "act":
                    continue
                act.wait_ge(s_job, n + 1)
                bank = psum[:, n % 8, :]
                if name == "ws":
                    nc.scalar.copy(wsT[:, arg], bank.rearrange("p (g q) -> p g q", q=P)).then_inc(s_free["act"], 1)
                else:
                    et, c = arg
                    c0, cn = CH[c]
                    if name == "q" and arg == (0, 0):
                        act.wait_ge(s_bq, 1)
                    dst = (q_tile(et) if name == "q" else kT[:, et, :])[:, c0:c0 + cn]
                    b = b_qk[:, et:et + 1] if name == "q" else b_qk[:, 4 + et:5 + et]
                    nc.scalar.activation(dst, bank[:, 0:cn], ACT.Identity, bias=b,
                                         scale=HD ** -0.5 if name == "q" else 1.0).then_inc(s_free["act"], 1)

            def split_high(step):
                h, (what, piece) = step // len(HIGH_STEPS), HIGH_STEPS[step % len(HIGH_STEPS)]
                c0, cn = PIECES[piece]
                here, cols = slice(HD * (h % 2), HD * (h % 2) + HD), slice(c0, c0 + cn)
                there = slice(HD - HD * (h % 2), 2 * HD - HD * (h % 2))
                if h >= 2 and step % len(HIGH_STEPS) == 0:
                    act.wait_ge(s_qk, HU * (h - 1))
                src = (q_tile(h // 2) if what == "q" else kT[:, h // 2, :])[here, cols]
                dst = (q_parts if what == "q" else k_high)[there if what == "k again" else here, h % 2, cols]
                nc.scalar.copy(dst, src).then_inc(s_sh, 1)

            act.wait_ge(s_free["act"], sum(e == "act" for _, _, e in jobs))
            act.wait_ge(s_job, len(jobs))
            for step in range(len(HIGH_STEPS)):
                split_high(step)

            for n in range(NU + 2):
                h, i = divmod(n, HU)
                if h + 1 < HEADS and 1 <= i <= len(HIGH_STEPS):
                    split_high(len(HIGH_STEPS) * (h + 1) + i - 1)
                if n >= 2:
                    m = n - 2
                    act.wait_ge(s_pt, m + 1)
                    if m >= 2:
                        act.wait_ge(s_pv, m - 1)
                    nk = glen[units[m][1]] // P
                    src = psum[:, 4:6, :].rearrange("p b (k c) -> p (b k) c", c=P)[:, 0:nk, :]
                    nc.scalar.copy(probsT[:, m % 2, 0:nk, :], src).then_inc(s_ptc, 1)
                if n < NU:
                    L = glen[units[n][1]]
                    act.wait_ge(s_scored, n + 1)
                    if n >= 3:
                        act.wait_ge(s_pt, n - 2)
                    nc.scalar.activation(probs[:, n % 3, 0:L], scored[:, n % 2, 0:L], ACT.Exp, bias=nmx[:, n % 4:n % 4 + 1],
                                         scale=1.0, accum_out=den[:, n % 8:n % 8 + 1]).then_inc(s_probs, 1)

            def cat_copy(t):
                act.wait_ge(s_catT, t + 1)
                if t >= 2:
                    act.wait_ge(s_mix, t - 1)
                nc.scalar.copy(catT[:, HI, t % 2], psum[:, 0:2, :].rearrange("p b (k c) -> p (b k) c", c=P)).then_inc(s_ch, 1)

            act.wait_ge(s_pv, NU)
            act.wait_ge(s_wout, 16)
            cat_copy(0)
            for k in range(KT):
                nc.scalar.copy(wout_hi[:, k, :], wout[:, k, :]).then_inc(s_oh, 1)
            for t in range(TILES + 1):
                if t >= 1:
                    m = t - 1
                    act.wait_ge(s_x1, m + 1)
                    if m >= 2:
                        act.wait_ge(s_x1st[m % 2], 32 * (m // 2))
                    nc.scalar.mul(ax1[:, m % 2], x1[:, m % 2], ALPHA).then_inc(s_ax1, 1)
                    act.wait_ge(s_x1T, m + 1)
                    if m >= 2:
                        act.wait_ge(s_log, m - 1)
                    nc.scalar.copy(x1T[:, m % 2], psum[:, 6:8, :].rearrange("p b (k c) -> p (b k) c", c=P)).then_inc(s_x1Tc, 1)
                if t + 1 < TILES:
                    cat_copy(t + 1)
                if t >= 1:
                    m = t - 1
                    act.wait_ge(s_smx, m + 1)
                    if m >= 2:
                        act.wait_ge(s_aff, m - 1)
                    nc.scalar.activation(aff_e[:, m % 2], psum[:, 6, 0:EXPERTS], ACT.Exp, bias=smx[:, m % 2:m % 2 + 1], scale=1.0,
                                         accum_out=ssum[:, m % 2:m % 2 + 1]).then_inc(s_sexp, 1)

            def xs_copy(e_done):
                act.wait_ge(s_xsT, e_done)
                for b in range(3):
                    nk = min(3, KT - 3 * b)
                    last = nc.scalar.copy(xs_parts[:, HI, 3 * b:3 * b + nk, :], psum[:, b, 0:nk * SLOTS].rearrange("p (k c) -> p k c", k=nk))
                last.then_inc(s_xsH, 1)

            def ys_copy(half, bank_s, bank_p, gate_s, gate_p):
                c = slice(512 * half, 512 * half + 512)
                nc.scalar.activation(ys[:, c], psum[:, bank_s, :], ACT.Copy, scale=gate_s)
                nc.scalar.activation(ys_p[0:CAP_P, c], psum[0:CAP_P, bank_p, :], ACT.Copy, scale=gate_p).then_inc(s_ys, 1)

            act.wait_ge(s_idx, 1)
            xs_copy(1)
            act.sem_inc(s_silu, 1)
            act.sem_inc(s_ys, 1)
            with act.Fori(0, EXPERTS) as e:
                for u in range(UNITS):
                    act.wait_ge(s_unit_in[u % RING], e * (16 * UNITS // RING) + 16 * (u // RING + 1))
                    act.wait_ge(s_unit, e * UNITS + (u + 1))
                    nc.scalar.copy(w_parts[:, HI, u % SPLIT, :], raw[:, u % RING, :]).then_inc(s_hi, 1)
                    if u % 4 == 3 and 7 <= u <= GU_UNITS + 3:
                        pr = (u - 7) // 4
                        act.wait_ge(s_gate, e * PAIRS + (pr + 2))
                        act.wait_ge(s_mul, e * PAIRS + max(pr, 1))
                        nc.scalar.activation(sg[:, pr % 2], gate_sum[:, pr % 2], ACT.Silu).then_inc(s_silu, 1)
                    if u % 4 == 1 and 9 <= u <= GU_UNITS + 5:
                        pr = (u - 9) // 4
                        act.wait_ge(s_mul, e * PAIRS + (pr + 2))
                        nc.scalar.copy(h_parts[:, HI, 2 * pr:2 * pr + 2, :], hid[:, pr % 2]).then_inc(s_hh, 1)
                    if u == 13:
                        act.wait_ge(s_yt, e * 2 + 1)
                        ys_copy(1, 4, 5, gates[:, 0, bass.ds(e, 1)], gates[0:CAP_P, 1, bass.ds(e, 1)])
                    if u == GU_UNITS + 7:
                        xs_copy(e + 2)
                    if u == GU_UNITS + DN_UNITS + 8:
                        act.wait_ge(s_yt, e * 2 + 2)
                        act.wait_ge(s_gi, e + 1)
                        ys_copy(0, 3, 0, gates[:, 0, bass.ds(e + 1, 1)], gates[0:CAP_P, 1, bass.ds(e + 1, 1)])
            def ys_high(half, g, n, rows):
                c = slice(512 * half, 512 * half + 512)
                nc.scalar.copy(ys_parts[0:n, HI, g, c], rows[0:n, c]).then_inc(s_yh, 1)

            act.wait_ge(s_ys, EXPERTS * 2 + 1)
            act.wait_ge(s_unit, EXPERTS * UNITS + SPLIT)
            ys_high(0, 0, CAP_S, ys)
            act.wait_ge(s_yt, EXPERTS * 2 + 1)
            ys_copy(1, 4, 5, gates[:, 0, EXPERTS:EXPERTS + 1], gates[0:CAP_P, 1, EXPERTS:EXPERTS + 1])
            act.wait_ge(s_ys, EXPERTS * 2 + 2)
            ys_high(1, 0, CAP_S, ys)
            ys_high(0, 1, CAP_P, ys_p)
            ys_high(1, 1, CAP_P, ys_p)
            for i in range(TILES):
                act.wait_ge(s_frs, i + 1)
                if i >= 5:
                    act.wait_ge(s_out[i % 5], 16 * (i // 5))
                nc.scalar.activation(fin[:, i % 5], psum[:, FIN_BANKS[i % 4]:FIN_BANKS[i % 4] + 2, :].rearrange("p b c -> p (b c)"),
                                     ACT.Identity, bias=nmr[:, i:i + 1], scale=rstd[:, i:i + 1]).then_inc(s_norm, 1)

        @block.vector
        def _(dve):
            chain = [0]

            def link(ins):
                chain[0] += 1
                ins.then_inc(s_dch, 1)
                dve.wait_ge(s_dch, chain[0])

            nc.vector.memset(table[N_BUCKETS:N_BUCKETS + 1, :], 1.0).then_inc(s_table1, 1)

            def gmlp_stats(t):
                dve.wait_ge(s_gelu, TILES + t + 1)
                if t:
                    dve.wait_ge(s_stat, t)
                link(nc.vector.bn_stats(stats[:, 0, :], vn[:, t, :]))
                nc.vector.bn_aggr(mv[:, t, :], stats[:, 0, :]).then_inc(s_stat, 1)

            def gmlp_norm(t):
                dve.wait_ge(s_rstd, t + 1)
                link(nc.vector.scalar_tensor_tensor(vn[:, t, :], vn[:, t, :], mv[:, t, 0:1], gln_g, ALU.subtract, ALU.mult))
                nc.vector.scalar_tensor_tensor(vn[:, t, :], vn[:, t, :], rstd[:, t:t + 1], gln_b, ALU.mult, ALU.add).then_inc(s_vn, 1)

            def low(out, whole, high):
                return nc.vector.tensor_tensor(out, whole, high.bitcast(F32), ALU.subtract)

            def split_win(u):
                dve.wait_ge(s_wh, u + 1)
                low(win_parts[:, LO, u % 2], win_raw[:, u % 2], win_parts[:, HI, u % 2]).then_inc(s_wl, 1)

            nat, unit = 0, 0
            for n, (name, arg, eng) in enumerate(jobs):
                if 2 <= unit < len(WUNITS) and n == unit_jobs[unit - 2] + 1:
                    split_win(unit)
                    unit += 1
                if eng != "dve":
                    continue
                dve.wait_ge(s_job, n + 1)
                bank = psum[:, n % 8, :]
                done = lambda ins: ins.then_inc(s_free["dve"], 1)
                if name == "rel":
                    done(nc.vector.tensor_copy(rel_bias[0:HEADS, arg * 512:(arg + 1) * 512], bank[0:HEADS, :]))
                elif name == "xT":
                    t, i = arg
                    dve.wait_ge(s_xh, n - 3)
                    ks, ts = slice(4 * i, 4 * i + 4), slice(t * P, (t + 1) * P)
                    done(low(x_parts[:, LO, ks, ts], bank.rearrange("p (k c) -> p k c", k=4), x_parts[:, HI, ks, ts]))
                    if arg == (TILES - 1, 1):
                        split_win(0)
                        split_win(1)
                        unit = 2
                elif name in ("gv", "gu"):
                    half, t = arg
                    cols = slice(half * W_COLS, (half + 1) * W_COLS)
                    if nat == 0:
                        dve.wait_ge(s_const, 64)
                    if nat >= 2:
                        dve.wait_ge(s_gelu, nat - 1)
                    done(nc.vector.tensor_tensor(pre[nat % 2][:, 0:W_COLS], bank[:, 0:W_COLS], rowb[:, 1 if name == "gv" else 0, cols], ALU.add))
                    if TILES + 1 <= nat <= 2 * TILES:
                        gmlp_stats(nat - TILES - 1)
                    if TILES + 2 <= nat <= 2 * TILES + 1:
                        gmlp_norm(nat - TILES - 2)
                    nat += 1
                elif name == "gm":
                    if arg == 0:
                        dve.wait_ge(s_bs, 32)
                        dve.wait_ge(s_gelu, 4 * TILES)
                    g = vn[:, arg, :]
                    link(nc.vector.tensor_tensor(g.rearrange("p (g c) -> p g c", c=HD), bank.rearrange("p (g c) -> p g c", c=HD),
                                                 b_s.unsqueeze(2).to_broadcast([P, 8, HD]), ALU.add))
                    done(nc.vector.tensor_tensor(gm[:, arg, :], gm[:, arg, :], g, ALU.mult))
                elif name == "v":
                    half, t = arg
                    cols = slice(half * W_COLS, (half + 1) * W_COLS)
                    done(nc.vector.tensor_tensor(v_rows[:, t, cols], bank[:, 0:W_COLS], v_bias[:, cols], ALU.add))

            def split_low(step):
                h, (what, piece) = step // len(LOW_STEPS), LOW_STEPS[step % len(LOW_STEPS)]
                c0, cn = PIECES[piece]
                here, cols = slice(HD * (h % 2), HD * (h % 2) + HD), slice(c0, c0 + cn)
                there = slice(HD - HD * (h % 2), 2 * HD - HD * (h % 2))
                dve.wait_ge(s_sh, len(HIGH_STEPS) * h + HIGH_STEPS.index((what, piece)) + 1)
                if what == "q":
                    low(q_parts[there, h % 2, cols], q_tile(h // 2)[here, cols], q_parts[here, h % 2, cols]).then_inc(s_sl, 1)
                else:
                    low(k_low[here, h % 2, cols], kT[here, h // 2, cols], k_high[here, h % 2, cols]).then_inc(s_sl, 1)

            for step in range(len(LOW_STEPS)):
                split_low(step)

            for n in range(NU + 4):
                h, i = divmod(n, HU)
                if h + 1 < HEADS and 4 <= i < 4 + len(LOW_STEPS):
                    split_low(len(LOW_STEPS) * (h + 1) + i - 4)
                if n < NU:
                    h, g, qt = units[n]
                    L = glen[g]
                    dve.wait_ge(s_qk, n + 1)
                    if n >= 2:
                        dve.wait_ge(s_probs, n - 1)
                    if g == 0 and qt == 0:
                        dve.wait_ge(s_relT[h % 2], 16 * (h // 2 + 1))
                    hi = qt * P + L_SAMPLE - 1
                    lo = hi - (L - 1)
                    bias = relT[:, h % 2, lo:hi + 1][:, ::-1]
                    src = psum[:, 2 * (n % 2):2 * (n % 2) + 2, :].rearrange("p b c -> p (b c)")[:, 0:L]
                    link(nc.vector.tensor_tensor_reduce(out=scored[:, n % 2, 0:L], in0=src, in1=bias, scale=1.0, scalar=-3e38,
                                                        op0=ALU.add, op1=ALU.max, accum_out=mx[:, n % 4:n % 4 + 1]))
                    nc.vector.tensor_scalar(nmx[:, n % 4:n % 4 + 1], mx[:, n % 4:n % 4 + 1], -1.0, None, ALU.mult).then_inc(s_scored, 1)
                if n >= 4:
                    m = n - 4
                    h, g, qt = units[m]
                    dve.wait_ge(s_pv, m + 1)
                    if m >= 2:
                        dve.wait_ge(s_att, m - 1)
                    link(nc.vector.reciprocal(rden[:, m % 2:m % 2 + 1], den[:, m % 8:m % 8 + 1]))
                    nc.vector.tensor_scalar(att[:, gtile[g] + qt, h * HD:(h + 1) * HD], psum[:, 6 + m % 2, 0:HD],
                                            rden[:, m % 2:m % 2 + 1], None,
                                            ALU.mult).then_inc(s_att, 1)


            def cat_low(t):
                dve.wait_ge(s_ch, t + 1)
                low(catT[:, LO, t % 2], psum[:, 0:2, :].rearrange("p b (k c) -> p (b k) c", c=P), catT[:, HI, t % 2]).then_inc(s_catTc, 1)

            def layer_norm_1(t):
                dve.wait_ge(s_mix, t + 1)
                dve.wait_ge(s_xa[t % 2], 16 * (t // 2 + 1))
                r = resid[:, t % 2]
                if t >= 2:
                    dve.wait_ge(s_x1, t - 1)
                link_res(nc.vector.scalar_tensor_tensor(r, x_again[:, t % 2], ALPHA, psum[:, 2 + 2 * (t % 2):4 + 2 * (t % 2), :]
                                                        .rearrange("p b c -> p (b c)"), ALU.mult, ALU.add), t)
                dve.wait_ge(s_stat, TILES + t)
                for i in range(2):
                    ins = nc.vector.bn_stats(stats[:, i, :], r[:, i * 512:(i + 1) * 512])
                link(ins)
                nc.vector.bn_aggr(mv[:, t, :], stats).then_inc(s_stat, 1)
                dve.wait_ge(s_rstd, TILES + t + 1)
                link(nc.vector.scalar_tensor_tensor(r, r, mv[:, t, 0:1], ln1_g, ALU.subtract, ALU.mult))
                if t >= 2:
                    dve.wait_ge(s_x1st[t % 2], 32 * (t // 2))
                    dve.wait_ge(s_ax1, t - 1)
                    dve.wait_ge(s_x1T, t - 1)
                nc.vector.scalar_tensor_tensor(x1[:, t % 2], r, rstd[:, t:t + 1], ln1_b, ALU.mult, ALU.add).then_inc(s_x1, 1)

            def link_res(ins, t):
                ins.then_inc(s_res, 1)
                dve.wait_ge(s_res, t + 1)

            def soft_max(t):
                dve.wait_ge(s_log, t + 1)
                if t:
                    dve.wait_ge(s_smx, t)
                link(nc.vector.reduce_max(lmx, psum[:, 6, 0:EXPERTS], AX_X))
                nc.vector.tensor_scalar(smx[:, t % 2:t % 2 + 1], lmx, -1.0, None, ALU.mult).then_inc(s_smx, 1)

            def soft_norm(t):
                dve.wait_ge(s_sexp, t + 1)
                if t >= 2:
                    dve.wait_ge(s_affT, t - 1)
                dve.wait_ge(s_aff, t) if t else dve.wait_ge(s_att, NU)
                link(nc.vector.reciprocal(rden[:, 0:1], ssum[:, t % 2:t % 2 + 1]))
                nc.vector.tensor_scalar(aff[:, t % 2], aff_e[:, t % 2], rden[:, 0:1], None, ALU.mult).then_inc(s_aff, 1)

            def aff_copy(t):
                dve.wait_ge(s_affT, t + 1)
                dst = aff_a[32:32 + EXPERTS, t * P:(t + 1) * P] if t < PT else aff_a[0:EXPERTS, (t - PT) * P:(t - PT + 1) * P]
                nc.vector.tensor_copy(dst, psum[0:EXPERTS, 7, 0:P]).then_inc(s_affTc, 1)

            dve.wait_ge(s_ln1, 48)
            cat_low(0)
            for k in range(KT):
                dve.wait_ge(s_oh, k + 1)
                if k >= 5:
                    dve.wait_ge(s_ol, k - 4)
                low(wout_lo[:, k, :], wout[:, k, :], wout_hi[:, k, :]).then_inc(s_ol, 1)
            dve.wait_ge(s_ol, KT)
            link(nc.vector.memset(aff_a[0:48, :], -1.0))
            for t in range(TILES + 2):
                if 2 <= t < TILES + 1:
                    aff_copy(t - 2)
                if t + 1 < TILES:
                    cat_low(t + 1)
                if t < TILES:
                    layer_norm_1(t)
                if 0 <= t - 1 < TILES:
                    soft_max(t - 1)
                    soft_norm(t - 1)
            aff_copy(TILES - 1)

            dve.wait_ge(s_affTc, TILES)
            cur, nxt = aff_a, aff_b
            for i in range(CAP_S // 8):
                v8 = top_val[0:48, 8 * i:8 * i + 8]
                link(nc.vector.max(v8, cur[0:48, :]))
                nc.vector.max_index(top_idx[0:48, 8 * i:8 * i + 8], v8, cur[0:48, :])
                link(nc.vector.match_replace(nxt[0:48, :], v8, cur[0:48, :], -1.0))
                cur, nxt = nxt, cur
            link(nc.vector.tensor_copy(top_idf[0:48, :], top_idx[0:48, :]))
            nc.vector.tensor_scalar(top_idf[0:EXPERTS, :], top_idf[0:EXPERTS, :], float(L_PROMPT), None, ALU.add).then_inc(s_top, 1)
            link(nc.vector.memset(gates, 0.0))
            link(nc.vector.memset(yT, 0.0))
            dve.wait_ge(s_topT, 1)
            for g in range(2):
                c = slice(32 * g, 32 * g + EXPERTS)
                nc.vector.tensor_copy(gates[:, g, 1:EXPERTS + 1], psum[:, 0, c])
                nc.vector.tensor_copy(idx[:, g, 0:EXPERTS], psum[:, 1, c])
                nc.vector.tensor_copy(idx[:, g, EXPERTS:EXPERTS + 1], psum[:, 1, c.stop - 1:c.stop])
                ins = nc.vector.tensor_copy(last_idx[:, g:g + 1], psum[:, 1, c.stop - 1:c.stop])
            ins.then_inc(s_idx, 1)
            dve.wait_ge(s_idx, 1)
            dve.wait_ge(s_numbers, 16)
            nc.vector.tensor_scalar(sel[:, L_PROMPT:], numbers[:, L_PROMPT:], last_idx[:, 0:1], None, ALU.is_equal)
            nc.vector.tensor_scalar(sel[0:CAP_P, 0:L_PROMPT], numbers[0:CAP_P, 0:L_PROMPT], last_idx[0:CAP_P, 1:2], None,
                                    ALU.is_equal).then_inc(s_sel, 1)

            def xs_low(count):
                dve.wait_ge(s_xsH, count)
                for b in range(3):
                    nk = min(3, KT - 3 * b)
                    ks = slice(3 * b, 3 * b + nk)
                    last = low(xs_parts[:, LO, ks, :], psum[:, b, 0:nk * SLOTS].rearrange("p (k c) -> p k c", k=nk), xs_parts[:, HI, ks, :])
                last.then_inc(s_xsL, 1)

            def both(out, banks):
                return nc.vector.reduce_sum(out, banks, AX_X)

            def y_copy(half, count):
                dve.wait_ge(s_unit, count)
                for i in range(4):
                    both(yT[:, 4 * half + i, :], psum[:, 4 + i, 0:2 * SLOTS].rearrange("p (c s) -> p s c", c=2)).then_inc(s_yT, 1)

            xs_low(1)
            dve.sem_inc(s_gate, 1)
            dve.sem_inc(s_mul, 1)
            dve.sem_inc(s_hid, 1)
            with dve.Fori(0, EXPERTS) as e:
                for u in range(UNITS):
                    dve.wait_ge(s_hi, e * UNITS + (u + 1))
                    low(w_parts[:, LO, u % SPLIT, :], raw[:, u % RING, :], w_parts[:, HI, u % SPLIT, :]).then_inc(s_lo, 1)
                    if u == 4:
                        y_copy(1, e * UNITS + SPLIT)
                    if u % 4 == 2 and 6 <= u <= GU_UNITS + 2:
                        pr = (u - 6) // 4
                        dve.wait_ge(s_unit, e * UNITS + (4 * pr + 2 + SPLIT))
                        dve.wait_ge(s_silu, e * PAIRS + max(pr, 1))
                        both(gate_sum[:, pr % 2], psum[:, 0:2, 0:2 * SLOTS].rearrange("p j (c s) -> p j s c", c=2)).then_inc(s_gate, 1)
                    if u % 4 == 0 and 8 <= u <= GU_UNITS + 4:
                        pr = (u - 8) // 4
                        dve.wait_ge(s_unit, e * UNITS + (4 * pr + 4 + SPLIT))
                        dve.wait_ge(s_mul, e * PAIRS + (pr + 1))
                        both(up_sum, psum[:, 2:4, 0:2 * SLOTS].rearrange("p j (c s) -> p j s c", c=2)).then_inc(s_up, 1)
                        dve.wait_ge(s_up, e * PAIRS + (pr + 1))
                        dve.wait_ge(s_silu, e * PAIRS + (pr + 2))
                        dve.wait_ge(s_hid, e * PAIRS + max(pr, 1))
                        nc.vector.tensor_tensor(hid[:, pr % 2], sg[:, pr % 2], up_sum, ALU.mult).then_inc(s_mul, 1)
                    if u % 4 == 2 and 10 <= u <= GU_UNITS + 6:
                        pr = (u - 10) // 4
                        dve.wait_ge(s_hh, e * PAIRS + (pr + 1))
                        low(h_parts[:, LO, 2 * pr:2 * pr + 2, :], hid[:, pr % 2], h_parts[:, HI, 2 * pr:2 * pr + 2, :]).then_inc(s_hid, 1)
                    if u == GU_UNITS + 8:
                        xs_low(e + 2)
                    if u == GU_UNITS + DN_UNITS + 4:
                        y_copy(0, e * UNITS + (GU_UNITS + DN_UNITS + SPLIT))
            y_copy(1, EXPERTS * UNITS + SPLIT)

            for n in range(4):
                g, half = divmod(n, 2)
                rows, c = slice(0, (CAP_S, CAP_P)[g]), slice(512 * half, 512 * half + 512)
                dve.wait_ge(s_yh, n + 1)
                low(ys_parts[rows, LO, g, c], (ys, ys_p)[g][rows, c], ys_parts[rows, HI, g, c]).then_inc(s_yl, 1)

            dve.wait_ge(s_ln2, 32)
            for i in range(TILES + 2):
                if i < TILES:
                    dve.wait_ge(s_sum, i + 1)
                    if i >= 2:
                        dve.wait_ge(s_fst, i - 1)
                    for j in range(2):
                        ins = nc.vector.bn_stats(fin_stats[:, i % 2, j, :], psum[:, FIN_BANKS[i % 4] + j, :])
                    link(ins)
                    nc.vector.bn_aggr(mv[:, i, :], fin_stats[:, i % 2]).then_inc(s_fst, 1)
                if i >= 2:
                    m = i - 2
                    dve.wait_ge(s_norm, m + 1)
                    nc.vector.tensor_tensor(fin[:, m % 5], fin[:, m % 5], ln2_g, ALU.mult).then_inc(s_gain, 1)

        @block.gpsimd
        def _(pool):
            chain = [0]

            def link(ins):
                chain[0] += 1
                ins.then_inc(s_pool, 1)
                pool.wait_ge(s_pool, chain[0])

            nc.gpsimd.memset(ident, 0.0).then_inc(s_ident, 1)
            link(nc.gpsimd.memset(half_neg, -0.5))
            pool.wait_ge(s_ident, 1)
            nc.gpsimd.affine_select(out=ident, in_=ident, compare_op=ALU.not_equal, fill=1.0, base=0,
                                    pattern=[[-1, P]], channel_multiplier=1).then_inc(s_ident, 1)
            def rstds(lo, hi):
                for n in range(lo, hi):
                    t = n % TILES
                    pool.wait_ge(s_stat, n + 1)
                    if n:
                        pool.wait_ge(s_rstd, n)
                    link(nc.gpsimd.tensor_scalar(veps, mv[:, t, 1:2], EPS, None, ALU.add))
                    nc.gpsimd.tensor_tensor(rstd[:, t:t + 1], veps, half_neg, ALU.pow).then_inc(s_rstd, 1)

            rstds(0, 2 * TILES)

            def gather(e, copied, count):
                nc.gpsimd.tensor_copy(idx_g, idx[:, :, bass.ds(e, 1)].rearrange("p g o -> p (g o)")).then_inc(copied, 1)
                pool.wait_ge(s_idx, 1)
                pool.wait_ge(copied, count)
                pool.indirect_dma_start(xs, None, x1_d, bass.IndirectOffsetOnAxis(ap=idx_g[:, 0:1], axis=0)).then_inc(s_gath, 16)
                pool.indirect_dma_start(xs_p[0:CAP_P, :], None, x1_d,
                                        bass.IndirectOffsetOnAxis(ap=idx_g[0:CAP_P, 1:2], axis=0)).then_inc(s_gath, 16)

            for i in range(2):
                pool.wait_ge(s_x1st[i], 32 * (TILES // 2))
            pool.wait_ge(s_idx, 1)
            gather(0, s_gi0, 1)
            pool.wait_ge(s_xsT, 1)
            gather(1, s_gi, 1)

            def scatter(e):
                pool.wait_ge(s_gi, e + 1)
                pool.wait_ge(s_ys, e * 2 + 4)
                nc.gpsimd.tensor_copy(idx_s, idx[:, :, bass.ds(e, 1)].rearrange("p g o -> p (g o)")).then_inc(s_si, 1)
                pool.wait_ge(s_idx, 1)
                pool.wait_ge(s_si, e + 1)
                pool.indirect_dma_start(acc_d, bass.IndirectOffsetOnAxis(ap=idx_s[:, 0:1], axis=0), ys, None,
                                        compute_op=ALU.add).then_inc(s_scat, 16)
                pool.indirect_dma_start(acc_d, bass.IndirectOffsetOnAxis(ap=idx_s[0:CAP_P, 1:2], axis=0), ys_p[0:CAP_P, :], None,
                                        compute_op=ALU.add).then_inc(s_scat, 16)

            with pool.Fori(0, EXPERTS - 1) as e:
                scatter(e)
                pool.wait_ge(s_scat, e * 32 + 32)
                pool.wait_ge(s_xsT, e + 2)
                gather(e + 2, s_gi, e + 2)

            pool.wait_ge(s_ln2, 32)
            for i in range(TILES + 3):
                if i < TILES:
                    pool.wait_ge(s_fst, i + 1)
                    link(nc.gpsimd.tensor_scalar(veps, mv[:, i, 1:2], EPS, None, ALU.add))
                    link(nc.gpsimd.tensor_tensor(rstd[:, i:i + 1], veps, half_neg, ALU.pow))
                    nc.gpsimd.tensor_scalar(nmr[:, i:i + 1], mv[:, i, 0:1], rstd[:, i:i + 1], -1.0, ALU.mult, ALU.mult).then_inc(s_frs, 1)
                if i >= 3:
                    m = i - 3
                    pool.wait_ge(s_gain, m + 1)
                    nc.gpsimd.tensor_tensor(fin[:, m % 5], fin[:, m % 5], ln2_b, ALU.add).then_inc(s_fin, 1)


NAMES = ["x_prompt", "x_sample", "rel_bias_table", "w_in", "b_in", "gmlp_ln_g", "gmlp_ln_b", "gmlp_w_s", "gmlp_b_s",
         "w_out", "ln1_g", "ln1_b", "w_router", "w_gate", "w_up", "w_down", "ln2_g", "ln2_b"]


def kernel(**inputs):
    import concourse.bacc as bacc
    from concourse.bass_utils import run_bass_kernel_spmd

    nc = bacc.Bacc("TRN2", target_bir_lowering=False, num_devices=1)
    arrays, aps = {}, {}
    constants = {"rel_rows": relative_rows(), "token_numbers": np.arange(TOKENS, dtype=np.float32)[None, :]}
    for name in NAMES + list(constants):
        x = constants[name] if name in constants else np.ascontiguousarray(inputs[name])
        arrays["in_" + name] = x
        aps[name] = nc.dram_tensor("in_" + name, x.shape, mybir.dt.from_np(x.dtype), kind="ExternalInput").ap()
    outs = [nc.dram_tensor(n, (1, length, D), F32, kind="ExternalOutput").ap()
            for n, length in (("y_prompt", L_PROMPT), ("y_sample", L_SAMPLE))]
    build(nc, aps, outs)
    r = run_bass_kernel_spmd(nc, [arrays], core_ids=[0]).results[0]
    return r["y_prompt"], r["y_sample"]
```
